# Optimizing a Trainium2 kernel written in Bass

```python
import math
import jax, jax.numpy as jnp
from jax import lax
import numpy as np

D_MODEL = 1024
BATCH = 1
SEQ = 256
DEPTH = 1
DEC_BATCH = 8
DEC_SEQ = 4
PAST_LEN = 2048
PAGE_SIZE = 128

HEAD_DIM = 64
N_ATT_HEADS = 12
ATT_WIDTH = N_ATT_HEADS * HEAD_DIM
CONV_GROUPS = 4
CONV_WIDTH = D_MODEL - ATT_WIDTH
CONV_K = 3
DILATION_PATTERNS = ((128, 1), (512, 4), (2048, 16))
WINDOW_MAX = max(w for w, _ in DILATION_PATTERNS)
Q_BLOCK = 128
ROPE_THETA = 10000.0
N_EXPERTS = 32
TOP_K = 4
D_FF = D_MODEL
SWIGLU_ALPHA = 1.702
SWIGLU_LIMIT = 7.0
MOE_BLOCK = 128
NORM_EPS = 1e-6
NEG_INF = -1e30
IN_PROJ_WIDTH = 3 * ATT_WIDTH + 3 * CONV_WIDTH
IN_SPLITS = (ATT_WIDTH, 2 * ATT_WIDTH, 3 * ATT_WIDTH,
             3 * ATT_WIDTH + CONV_WIDTH, 3 * ATT_WIDTH + 2 * CONV_WIDTH)

kernel_name = 'hybrid_dilated_attn_shortconv_moe_step'

def rmsnorm(x, g):
    xf = x.astype(jnp.float32)
    y = xf * lax.rsqrt(jnp.mean(xf * xf, axis=-1, keepdims=True) + NORM_EPS)
    return (y * g.astype(jnp.float32)).astype(x.dtype)

def rope(x, pos):
    half = HEAD_DIM // 2
    inv = ROPE_THETA ** (-jnp.arange(half, dtype=jnp.float32) / half)
    ang = pos.astype(jnp.float32)[:, None] * inv[None, :]
    cos = jnp.cos(ang)[None, :, None, :]
    sin = jnp.sin(ang)[None, :, None, :]
    xf = x.astype(jnp.float32)
    x1, x2 = xf[..., :half], xf[..., half:]
    return jnp.concatenate([x1 * cos - x2 * sin, x1 * sin + x2 * cos], axis=-1).astype(x.dtype)

def _combine(outs, lses):
    lse = jnp.stack(lses, 0)
    w = jax.nn.softmax(lse, axis=0)
    return jnp.einsum('p...h,p...he->...he', w, jnp.stack(outs, 0))

def dilated_attention_prompt(q, k, v):
    B, S = q.shape[0], q.shape[1]
    pad = jnp.zeros((B, WINDOW_MAX, N_ATT_HEADS, HEAD_DIM), k.dtype)
    k_pad = jnp.concatenate([pad, k], axis=1)
    v_pad = jnp.concatenate([pad, v], axis=1)
    n_blocks = S // Q_BLOCK

    def block(n):
        s0 = n * Q_BLOCK
        qb = lax.dynamic_slice_in_dim(q, s0, Q_BLOCK, axis=1).astype(jnp.float32)
        outs, lses = [], []
        for (w, d) in DILATION_PATTERNS:
            L = w + Q_BLOCK
            kb = lax.dynamic_slice_in_dim(k_pad, WINDOW_MAX + s0 - w, L, axis=1).astype(jnp.float32)
            vb = lax.dynamic_slice_in_dim(v_pad, WINDOW_MAX + s0 - w, L, axis=1).astype(jnp.float32)
            A, C = Q_BLOCK // d, L // d
            qr = qb.reshape(B, A, d, N_ATT_HEADS, HEAD_DIM)
            kr = kb.reshape(B, C, d, N_ATT_HEADS, HEAD_DIM)
            vr = vb.reshape(B, C, d, N_ATT_HEADS, HEAD_DIM)
            s = jnp.einsum('barhe,bcrhe->brhac', qr, kr)
            a_i = jnp.arange(A)[:, None]
            c_i = jnp.arange(C)[None, :]
            band = (c_i >= a_i) & (c_i <= a_i + w // d)
            key_pos = s0 - w + jnp.arange(C)[:, None] * d + jnp.arange(d)[None, :]
            mask = band[None, :, :] & (key_pos.T >= 0)[:, None, :]
            s = jnp.where(mask[None, :, None], s, NEG_INF)
            m = jnp.max(s, axis=-1, keepdims=True)
            p = jnp.exp(s - m)
            l = jnp.sum(p, axis=-1)
            l_t = jnp.transpose(l, (0, 3, 1, 2))
            o = jnp.einsum('brhac,bcrhe->barhe', p, vr) / l_t[..., None]
            lse = jnp.transpose(m[..., 0], (0, 3, 1, 2)) + jnp.log(l_t)
            outs.append(o.reshape(B, Q_BLOCK, N_ATT_HEADS, HEAD_DIM))
            lses.append(lse.reshape(B, Q_BLOCK, N_ATT_HEADS))
        return _combine(outs, lses)

    ob = lax.map(block, jnp.arange(n_blocks))
    return jnp.transpose(ob, (1, 0, 2, 3, 4)).reshape(B, S, N_ATT_HEADS, HEAD_DIM)

def dilated_attention_sample(q, k_all, v_all, n_past):
    T = q.shape[1]
    qf = q.astype(jnp.float32)
    outs, lses = [], []
    for (w, d) in DILATION_PATTERNS:
        offs = jnp.arange(w // d + 1) * d
        idx = n_past + jnp.arange(T)[:, None] - offs[None, :]
        valid = idx >= 0
        idx = jnp.maximum(idx, 0)
        kg = k_all[:, idx].astype(jnp.float32)
        vg = v_all[:, idx].astype(jnp.float32)
        s = jnp.einsum('bthe,btkhe->bthk', qf, kg)
        s = jnp.where(valid[None, :, None, :], s, NEG_INF)
        m = jnp.max(s, axis=-1, keepdims=True)
        p = jnp.exp(s - m)
        l = jnp.sum(p, axis=-1)
        o = jnp.einsum('bthk,btkhe->bthe', p, vg) / l[..., None]
        outs.append(o)
        lses.append(m[..., 0] + jnp.log(l))
    return _combine(outs, lses)

def _project(h, w_in):
    z = jnp.einsum('bsd,df->bsf', h, w_in)
    B, S = h.shape[0], h.shape[1]
    q, k, v, gb, gc, u = jnp.split(z, IN_SPLITS, axis=-1)
    shp = (B, S, N_ATT_HEADS, HEAD_DIM)
    return q.reshape(shp), k.reshape(shp), v.reshape(shp), gb, gc, u

def _short_conv(u_ext, conv_w):
    rhs = conv_w.astype(u_ext.dtype)[:, None, :]
    return lax.conv_general_dilated(u_ext, rhs, window_strides=(1,), padding='VALID',
                                    dimension_numbers=('NWC', 'WIO', 'NWC'),
                                    feature_group_count=CONV_WIDTH)

def _merge(att, conv_out, g_attn_out, g_conv_out, w_out):
    B, S = att.shape[0], att.shape[1]
    att = att.reshape(B, S, ATT_WIDTH)
    cat = jnp.concatenate([rmsnorm(att, g_attn_out), rmsnorm(conv_out, g_conv_out)], axis=-1)
    return jnp.einsum('bsf,fd->bsd', cat, w_out)

def _prompt_mixer(h, w_in, conv_w, g_attn_out, g_conv_out, w_out):
    S = h.shape[1]
    q, k, v, gb, gc, u = _project(h, w_in)
    pos = jnp.arange(S)
    q = rope(q, pos) * (HEAD_DIM ** -0.5)
    k = rope(k, pos)
    att = dilated_attention_prompt(q, k, v).astype(h.dtype)
    cu = gc * u
    cu_ext = jnp.pad(cu, ((0, 0), (CONV_K - 1, 0), (0, 0)))
    conv_out = gb * _short_conv(cu_ext, conv_w)
    y = _merge(att, conv_out, g_attn_out, g_conv_out, w_out)
    keep = min(WINDOW_MAX, S)
    return y, k[:, S - keep:], v[:, S - keep:], cu[:, S - (CONV_K - 1):]

def _sample_mixer(h, k_buf, v_buf, conv_buf, w_in, conv_w, g_attn_out, g_conv_out, w_out):
    T = h.shape[1]
    n_past = k_buf.shape[1]
    q, k, v, gb, gc, u = _project(h, w_in)
    pos = PAST_LEN + jnp.arange(T)
    q = rope(q, pos) * (HEAD_DIM ** -0.5)
    k = rope(k, pos)
    k_all = jnp.concatenate([k_buf.astype(k.dtype), k], axis=1)
    v_all = jnp.concatenate([v_buf.astype(v.dtype), v], axis=1)
    att = dilated_attention_sample(q, k_all, v_all, n_past).astype(h.dtype)
    cu = gc * u
    cu_ext = jnp.concatenate([conv_buf.astype(cu.dtype), cu], axis=1)
    conv_out = gb * _short_conv(cu_ext, conv_w)
    y = _merge(att, conv_out, g_attn_out, g_conv_out, w_out)
    return y, k, v, cu_ext[:, -(CONV_K - 1):]

def _moe(h, w_router, b_router, w_gate, b_gate, w_up, b_up, w_down, b_down):
    B, S, D = h.shape
    xt = h.reshape(B * S, D)
    N = xt.shape[0]
    logits = jnp.einsum('nd,de->ne', xt.astype(jnp.float32), w_router.astype(jnp.float32)) + b_router.astype(jnp.float32)
    top_v, top_i = lax.top_k(logits, TOP_K)
    gates = jax.nn.softmax(top_v, axis=-1)
    NK = N * TOP_K
    flat_e = top_i.reshape(NK)
    flat_t = jnp.arange(NK, dtype=jnp.int32) // TOP_K
    flat_g = gates.reshape(NK)
    order = jnp.argsort(flat_e)
    se = flat_e[order]
    counts = jnp.bincount(flat_e, length=N_EXPERTS)
    pcounts = (counts + MOE_BLOCK - 1) // MOE_BLOCK * MOE_BLOCK
    start = jnp.cumsum(counts) - counts
    pend = jnp.cumsum(pcounts)
    pstart = pend - pcounts
    dest = pstart[se] + jnp.arange(NK) - start[se]
    n_rows = -(-(NK + N_EXPERTS * (MOE_BLOCK - 1)) // MOE_BLOCK) * MOE_BLOCK
    n_blocks = n_rows // MOE_BLOCK
    row_tok = jnp.full((n_rows,), N, jnp.int32).at[dest].set(flat_t[order])
    row_g = jnp.zeros((n_rows,), jnp.float32).at[dest].set(flat_g[order])
    blk_e = jnp.minimum(jnp.searchsorted(pend, jnp.arange(n_blocks) * MOE_BLOCK, side='right'), N_EXPERTS - 1)
    x_pad = jnp.concatenate([xt, jnp.zeros((1, D), xt.dtype)], axis=0)
    xb = x_pad[row_tok].reshape(n_blocks, MOE_BLOCK, D)

    def expert_block(args):
        xblk, e = args
        g = xblk @ w_gate[e] + b_gate[e]
        u = xblk @ w_up[e] + b_up[e]
        g = jnp.minimum(g, SWIGLU_LIMIT)
        u = jnp.clip(u, -SWIGLU_LIMIT, SWIGLU_LIMIT)
        act = (u + 1) * g * jax.nn.sigmoid(SWIGLU_ALPHA * g)
        return act @ w_down[e] + b_down[e]

    yb = lax.map(expert_block, (xb, blk_e)).reshape(n_rows, D)
    y = jax.ops.segment_sum(yb.astype(jnp.float32) * row_g[:, None], row_tok, num_segments=N + 1)[:N]
    return y.astype(h.dtype).reshape(B, S, D)

def _modulations(c, w_ada, b_ada):
    m = jnp.einsum('bd,df->bf', jax.nn.silu(c), w_ada) + b_ada
    return jnp.split(m[:, None, :], 6, axis=-1)

def _modulate(x, g, shift, scale):
    return rmsnorm(x, g) * (1 + scale) + shift

def setup_inputs(seed: int = 0) -> dict:
    key = jax.random.key(seed)
    ks = jax.random.split(key, 32)
    f32 = jnp.float32
    wbuf = min(WINDOW_MAX, PAST_LEN)

    def nrm(k, shape, scale=1.0):
        return jax.random.normal(k, shape, f32) * scale

    L = DEPTH
    return {
        'x_prompt': nrm(ks[0], (BATCH, SEQ, D_MODEL)),
        'x_sample': nrm(ks[1], (DEC_BATCH, DEC_SEQ, D_MODEL)),
        'cache_k': nrm(ks[2], (L, DEC_BATCH, wbuf, N_ATT_HEADS, HEAD_DIM)),
        'cache_v': nrm(ks[3], (L, DEC_BATCH, wbuf, N_ATT_HEADS, HEAD_DIM)),
        'state_conv': nrm(ks[4], (L, DEC_BATCH, CONV_K - 1, CONV_WIDTH)),
        'c_prompt': nrm(ks[5], (BATCH, D_MODEL)),
        'c_sample': nrm(ks[6], (DEC_BATCH, D_MODEL)),
        'w_ada': nrm(ks[7], (L, D_MODEL, 6 * D_MODEL), D_MODEL ** -0.5),
        'b_ada': nrm(ks[8], (L, 6 * D_MODEL), 0.02),
        'g_norm_mix': 1.0 + nrm(ks[9], (L, D_MODEL), 0.02),
        'w_in': nrm(ks[10], (L, D_MODEL, IN_PROJ_WIDTH), D_MODEL ** -0.5),
        'conv_w': nrm(ks[11], (L, CONV_K, CONV_WIDTH), CONV_K ** -0.5),
        'g_attn_out': 1.0 + nrm(ks[12], (L, ATT_WIDTH), 0.02),
        'g_conv_out': 1.0 + nrm(ks[13], (L, CONV_WIDTH), 0.02),
        'w_out': nrm(ks[14], (L, D_MODEL, D_MODEL), D_MODEL ** -0.5),
        'g_norm_ffn': 1.0 + nrm(ks[15], (L, D_MODEL), 0.02),
        'w_router': nrm(ks[16], (L, D_MODEL, N_EXPERTS), D_MODEL ** -0.5),
        'b_router': nrm(ks[17], (L, N_EXPERTS), 0.01),
        'w_gate': nrm(ks[18], (L, N_EXPERTS, D_MODEL, D_FF), D_MODEL ** -0.5),
        'b_gate': nrm(ks[19], (L, N_EXPERTS, D_FF), 0.01),
        'w_up': nrm(ks[20], (L, N_EXPERTS, D_MODEL, D_FF), D_MODEL ** -0.5),
        'b_up': nrm(ks[21], (L, N_EXPERTS, D_FF), 0.01),
        'w_down': nrm(ks[22], (L, N_EXPERTS, D_FF, D_MODEL), D_FF ** -0.5),
        'b_down': nrm(ks[23], (L, N_EXPERTS, D_MODEL), 0.01),
        'g_final': 1.0 + nrm(ks[24], (D_MODEL,), 0.02),
    }

def reference(x_prompt, x_sample, cache_k, cache_v, state_conv, c_prompt, c_sample,
              w_ada, b_ada, g_norm_mix, w_in, conv_w, g_attn_out, g_conv_out, w_out,
              g_norm_ffn, w_router, b_router, w_gate, b_gate, w_up, b_up, w_down, b_down,
              g_final):
    xp, xs = x_prompt, x_sample
    kp_l, vp_l, cp_l, ks_l, vs_l, cs_l = [], [], [], [], [], []
    for l in range(DEPTH):
        moe_p = (w_router[l], b_router[l], w_gate[l], b_gate[l], w_up[l], b_up[l], w_down[l], b_down[l])
        mix_p = (w_in[l], conv_w[l], g_attn_out[l], g_conv_out[l], w_out[l])
        sh1, sc1, gt1, sh2, sc2, gt2 = _modulations(c_prompt, w_ada[l], b_ada[l])
        mix, kp, vp, cp = _prompt_mixer(_modulate(xp, g_norm_mix[l], sh1, sc1), *mix_p)
        xp = xp + gt1 * mix
        xp = xp + gt2 * _moe(_modulate(xp, g_norm_ffn[l], sh2, sc2), *moe_p)
        sh1, sc1, gt1, sh2, sc2, gt2 = _modulations(c_sample, w_ada[l], b_ada[l])
        mix, ksn, vsn, csn = _sample_mixer(_modulate(xs, g_norm_mix[l], sh1, sc1),
                                           cache_k[l], cache_v[l], state_conv[l], *mix_p)
        xs = xs + gt1 * mix
        xs = xs + gt2 * _moe(_modulate(xs, g_norm_ffn[l], sh2, sc2), *moe_p)
        kp_l.append(kp); vp_l.append(vp); cp_l.append(cp)
        ks_l.append(ksn); vs_l.append(vsn); cs_l.append(csn)
    y_prompt = rmsnorm(xp, g_final)
    y_sample = rmsnorm(xs, g_final)
    return (y_prompt, y_sample,
            jnp.stack(kp_l, 0), jnp.stack(vp_l, 0), jnp.stack(cp_l, 0),
            jnp.stack(ks_l, 0), jnp.stack(vs_l, 0), jnp.stack(cs_l, 0))


_drawn_inputs = setup_inputs


def setup_inputs(seed=0):
    import zlib

    import numpy as np

    out = dict(_drawn_inputs(seed))
    spreads = {}
    factors = {'g_conv_out': 3.043,
     'b_router': 4.713,
     'b_gate': 21.771,
     'b_up': 27.427,
     'b_down': 25.168,
     'g_final': 8.153,
     'g_attn_out': 3.022}
    for name, (base, spread) in spreads.items():
        noise = np.random.default_rng([zlib.crc32(name.encode()), seed]).standard_normal(out[name].shape)
        drawn = base * np.exp(spread * noise) if base else spread * noise
        out[name] = __import__('jax').numpy.asarray(drawn.astype(out[name].dtype))
    for name, factor in factors.items():
        out[name] = (out[name] * factor).astype(out[name].dtype)
    return out
```

```python
import math
from contextlib import ExitStack

import concourse.bass as bass
from concourse import mybir

F32 = mybir.dt.float32
I32 = mybir.dt.int32
U32 = mybir.dt.uint32
ALU = mybir.AluOpType
ACT = mybir.ActivationFunctionType
AX = mybir.AxisListType
ds = bass.ds

P = 128
D = 1024
KD = D // P
SEQ = 256
NSEQ = 8
TS = 4
NSAMP = NSEQ * TS
NT = SEQ + NSAMP
HEADS = 12
HD = 64
PAIRS = HEADS // 2
ATT = HEADS * HD
CONV = D - ATT
KA, KC = ATT // P, CONV // P
NIN = 3 * ATT + 3 * CONV
PAST = 2048
NEXP = 32
TOPK = 4
EPS = 1e-6
NEG = -1e30
LIMIT = 7.0
ALPHA = 1.702
SCALE = HD ** -0.5

RECENT = 4
CHUNKS = RECENT + (PAST - 512) // 16 * 4 // P
KEYS = CHUNKS * P
SETS = 4
HPS = HEADS // SETS
QR = HPS * TS
HALF_D = CHUNKS - 2

SLOTS = 12
PIECE = KD * 256
ADA_COLS = 2 * D
ADA_PIECES = 6 * KD * D // ADA_COLS
IN_PIECES = NIN // 256
OUT_PIECES = D // 256
IN0 = KD
ADA0 = IN0 + IN_PIECES
OUT0 = ADA0 + ADA_PIECES - KD
FRONT_PIECES = OUT0 + OUT_PIECES
EXP_PIECES = 12
EARLY = 8

WIDTHS = tuple(range(32, NT + 1, 32))
TOK_TILES = ((0, 128), (128, 128), (256, 32))


UNITS = 24


def slot_tiles(n):
    sizes = [32] * (n % 64 // 32) + [64] * (n % P // 64) + [P] * (n // P)
    return [(sum(sizes[:i]), m) for i, m in enumerate(sizes)]


def gather_width(n):
    return max(n, P)


def gather_chunks(n):
    return 4 if n <= P else 2 if n <= 256 else 1


def program(nc, x_prompt, x_sample, cache_k, cache_v, state_conv, c_prompt, c_sample,
            w_ada, b_ada, g_norm_mix, w_in, conv_w, g_attn_out, g_conv_out, w_out,
            g_norm_ffn, w_router, b_router, w_gate, b_gate, w_up, b_up, w_down, b_down, g_final,
            c_ident, c_tri, c_iota, c_rope, c_lcp, c_lcs, c_lcn,
            y_prompt, y_sample, k_prompt, v_prompt, conv_prompt, k_sample, v_sample, conv_sample):
    ctx = ExitStack()
    with ctx:
        def sb(name, shape, dt=F32):
            return ctx.enter_context(nc.sbuf_tensor(name, shape, dt))

        def sem(name):
            return ctx.enter_context(nc.semaphore(name))

        ring = sb("ring", [P, SLOTS, PIECE])
        xT = sb("xT", [P, KD, NT])
        hT = sb("hT", [P, KD, NT])
        NA = (2 * CHUNKS * ATT) + 3 * 3 * ATT + KD * NT
        arena = sb("arena", [P, NA])

        def view(off, *shape):
            n = math.prod(shape)
            a = arena[:, off:off + n]
            if len(shape) == 2:
                a = a.rearrange("p (a b) -> p a b", b=shape[1])
            if len(shape) == 3:
                a = a.rearrange("p (a b c) -> p a b c", b=shape[1], c=shape[2])
            return a

        o_k, o_v = 0, CHUNKS * ATT
        o_z = 2 * CHUNKS * ATT
        o_s = o_z + 9 * ATT
        K = view(o_k, CHUNKS, ATT)
        V = view(o_v, CHUNKS, ATT)
        Z = view(o_z, 3, 3 * ATT)
        scratch = view(o_s, KD, NT)
        xtok = view(o_z, 3, D)
        mod_rows = view(o_s + 1536, 512)
        crow = view(o_z + 3 * D, D)
        csig = view(o_v, D)
        vrows = view(o_z + 4 * D, P)
        srows = view(o_z + 4 * D + P, CONV)
        rstd = view(o_k, NT)
        rstd_c = view(o_k + NT, NT)
        rope1 = view(o_v, ATT)
        rope2 = view(o_v + ATT, ATT)
        BCU = view(o_s, 3 * KC, NT)
        CES = view(o_s + 3 * KC * NT, KC, NSEQ * 6)
        NCS = 2 + 2 * NSEQ
        CO = view(o_s + 3 * KC * NT + KC * NSEQ * 6, KC, NCS)
        COT = view(o_s + 3 * KC * NT + KC * NSEQ * 6 + KC * NCS, CONV)
        pP = [view(o_s, 384), view(o_s + 384, 384), view(o_z + 2 * 3 * ATT, 384)]
        pPT = [view(o_s + 768 + 384 * b, 384) for b in range(2)]
        KT = [view(o_s + ATT * b, PAIRS, P) for b in range(2)]
        sP = view(o_z + 2 * 3 * ATT, KEYS + NSAMP)
        PT = view(o_z, CHUNKS + 1, P)
        qb = view(o_z + (CHUNKS + 1) * P, 8, 32)
        o_sb = view(o_z + (CHUNKS + 1) * P + 256, HPS * HD)
        qb_all = view(o_z + 3 * ATT, NSEQ, 8 * QR)
        o = 0
        h2tok = view(o, 3, D); o += 3 * D
        acc = view(o, KD, NT); o += KD * NT
        ye = view(o, 3, D)
        brow = [view(o + D * b, D) for b in range(3)]
        o += 3 * D
        gate_rows, up_rows = view(o, D), view(o + D, D)
        o_y = o; o += 2 * D
        bd = {32: [view(o, 4, NT)], 64: [view(o + 4 * NT, 2, NT)],
              128: [view(o + 6 * NT, 1, NT), view(o + 7 * NT, 1, NT)]}
        bd_all = view(o, KD * NT); o += KD * NT
        Poh = view(o, 3 * NT); o += 3 * NT
        Pg = view(o, 3, 3 * P); o += 9 * P
        bgT = view(o, KD, NEXP); o += KD * NEXP
        buT = view(o, KD, NEXP); o += KD * NEXP
        tg = view(o, 512); o += 512
        tu = view(o, 512); o += 512
        sg = view(o, 512); o += 512
        iota = view(o, NT); o += NT
        G = view(o, 3, NEXP); o += 3 * NEXP
        posm = view(o, 3, NEXP); o += 3 * NEXP
        cnt = view(o, NEXP); o += NEXP
        rstd2 = view(o, NT)
        assert o + NT <= o_s, (o + NT, o_s)
        o = o_y
        wr = view(o, KD, NEXP); o += KD * NEXP
        GT = view(o, NT); o += NT
        tri = view(o, P); o += P
        logit = view(o, 3, NEXP); o += 3 * NEXP
        top8 = view(o, 3, 8); o += 24
        idx8 = view(o, 3, 8); o += 24
        idxf = view(o, 3, TOPK); o += 3 * TOPK
        gates = view(o, 3, TOPK); o += 3 * TOPK
        gsum = view(o, 4); o += 4
        eq4 = view(o, 3 * TOPK * NEXP); o += 3 * TOPK * NEXP
        sel = view(o, 3, NEXP); o += 3 * NEXP
        brrow = view(o, NEXP); o += NEXP
        assert o <= o_y + 2 * D
        xe = view(o_s, KD * NT)
        actT = hT[:, :, :].rearrange("p k n -> p (k n)")
        ytok = view(0, 3, D)

        ident = sb("ident", [P, P])
        ones = sb("ones", [P, P])
        vec = sb("vec", [P, 86])
        mods = sb("mods", [P, 48, 9])
        gs1 = sb("gs1", [P, KD, 9])
        gs2 = sb("gs2", [P, KD, 9])
        cT = sb("cT", [P, KD, 32])
        rope = sb("rope", [P, 3, 2, HD])
        lcp = sb("lcp", [P, 384])
        lcs = sb("lcs", [P, KEYS])
        lcn = sb("lcn", [P, NSEQ, NSAMP])
        qTs = sb("qTs", [P, PAIRS, NSAMP])
        kTs = sb("kTs", [P, PAIRS, NSAMP])
        cst = sb("cst", [P, 2 * NSEQ * KC])
        stat = sb("stat", [P, 16])
        eps = sb("eps", [P, 1])
        ps = ctx.enter_context(nc.psum_tensor("ps", [P, 8, 512], F32))

        g_mix, g_ffn, g_fin = vec[:, 48:56], vec[:, 56:64], vec[:, 64:72]
        g_cat = vec[:, 72:80]
        taps = vec[:, 80:86]

        piece_in = [sem(f"piece_in{s}") for s in range(SLOTS)]
        pieces_used = sem("pieces_used")
        pe_passed = sem("pe_passed")
        in_rows = sem("in_rows")
        in_x = sem("in_x")
        in_tab = sem("in_tab")
        in_moe = sem("in_moe")
        mods_copied, mods_T, mods_ready, cT_zero = (sem(n) for n in (
            "mods_copied", "mods_T", "mods_ready", "cT_zero"))
        h2_scaled = sem("h2_scaled")
        s_max = sem("s_max")
        weights_used = sem("weights_used")
        logits_T, logits_copied = sem("logits_T"), sem("logits_copied")
        sqrt_loaded = sem("sqrt_loaded")
        k_in = [sem(f"k_in{c}") for c in range(CHUNKS)]
        v_in = sem("v_in")
        k_used = sem("k_used")
        v_used = sem("v_used")
        out_kv = sem("out_kv")
        out_end = sem("out_end")
        dve_step = sem("dve_step")
        (vec_T, vec_copied, x_T, x_copied, silu, c_T, c_copied, c_sig,
         ones_set, x_sq, cat_sq, x1_sq, x2_sq, x_ss, att_ss, conv_ss,
         x1_ss, x2_ss, x_std, att_std, conv_std, x1_std, x2_std, h_ready,
         rope_done, qk_samp_T, q_blocks_set, qk_T, qk_copied, conv_rows_T, conv_rows, conv_last,
         conv_done, p_scores_made, p_masked, p_max, p_exped, p_normed, p_T, p_T_copied,
         p_out_made, p_out_copied, cat_ready, x1_ready, mix_made, bias_T, bias_copied, h2_ready,
         logits_made, h2_T, h2_copied, selected, places_made, gates_T, acc0_made, counts_ready,
         gates_less_max, gates_exp, x2_ready, y_ready, y_T, y_copied, z_made, z_copied,
         bcu_made, bcu_copied, k_stored, conv_stored) = (sem(n) for n in (
            "vec_T", "vec_copied", "x_T", "x_copied", "silu", "c_T", "c_copied", "c_sig",
            "ones_set", "x_sq", "cat_sq", "x1_sq", "x2_sq", "x_ss", "att_ss", "conv_ss",
            "x1_ss", "x2_ss", "x_std", "att_std", "conv_std", "x1_std", "x2_std", "h_ready",
            "rope_done", "qk_samp_T", "q_blocks_set", "qk_T", "qk_copied", "conv_rows_T", "conv_rows", "conv_last",
            "conv_done", "p_scores_made", "p_masked", "p_max", "p_exped", "p_normed", "p_T", "p_T_copied",
            "p_out_made", "p_out_copied", "cat_ready", "x1_ready", "mix_made", "bias_T", "bias_copied", "h2_ready",
            "logits_made", "h2_T", "h2_copied", "selected", "places_made", "gates_T", "acc0_made", "counts_ready",
            "gates_less_max", "gates_exp", "x2_ready", "y_ready", "y_T", "y_copied", "z_made", "z_copied",
            "bcu_made", "bcu_copied", "k_stored", "conv_stored"))

        kt_copied_a, kt_copied_d = sem("kt_copied_a"), sem("kt_copied_d")
        st_made, qb_zero, qb_made, qb_ready, s_made, s_masked, s_neg, s_exp, s_recip = (sem(n) for n in (
            "st_made", "qb_zero", "qb_made", "qb_ready", "s_made", "s_masked", "s_neg", "s_exp", "s_recip"))
        pt_made, pt_copied, o_scaled, o_T, o_copied = (sem(n) for n in (
            "pt_made", "pt_copied", "o_scaled", "o_T", "o_copied"))
        onehot, onehot_g = sem("onehot"), sem("onehot_g")
        hot_copies = sem("hot_copies")
        gathered, xe_ready = sem("gathered"), sem("xe_ready")
        hot_T_made, hot_T_ready = sem("hot_T_made"), sem("hot_T_ready")
        gate_made, up_made, gate_copied, up_copied, gate_T, up_T = (sem(n) for n in (
            "gate_made", "up_made", "gate_copied", "up_copied", "gate_T", "up_T"))
        g_biased, g_clipped, g_sig, u_biased, u_clipped, glu, act_ready = (sem(n) for n in (
            "g_biased", "g_clipped", "g_sig", "u_biased", "u_clipped", "glu", "act_ready"))
        down_made, ye_ready = sem("down_made"), sem("ye_ready")
        comb_made, acc_ready = sem("comb_made"), sem("acc_ready")
        moe_zeros = sem("moe_zeros")

        counts = {}

        def step(ins, signal, by=1):
            ins.then_inc(signal, by)
            counts[signal.name] = counts.get(signal.name, 0) + by
            return counts[signal.name]

        block = ctx.enter_context(nc.Block())

        def arrived(eng, n):
            eng.wait_ge(piece_in[n % SLOTS], 16 * (n // SLOTS + 1))

        def slot_w(n, rows=False):
            a = ring[:, n % SLOTS, :]
            return a.rearrange("p (k c) -> p k c", c=D if rows else 256)

        def moe_slot(j):
            return (FRONT_PIECES + j) % SLOTS

        GATE, UP, DOWN = range(0, 4), range(4, 8), range(8, 12)

        def rows_T_banks(N, i):
            return (0, 2) if i == len(slot_tiles(N)) - 1 else (6, 4)

        def comb_bank(c):
            return (6, 7, 4, 5)[c % 4]

        def bd_tile(m, i):
            return bd[m][i % len(bd[m])]

        def by_width(eng, n, body):
            def pick(i):
                if i == len(WIDTHS) - 1:
                    body(WIDTHS[i])
                    return
                with eng.If(n < WIDTHS[i] + 1):
                    body(WIDTHS[i])
                with eng.Else():
                    pick(i + 1)
            pick(0)

        def unit(n):
            return UNITS // len(slot_tiles(n))

        def parts(m):
            return max(1, KD * m // 512)

        def bank_pair(b, w):
            return ps[:, b:b + 2, :].rearrange("p b c -> p (b c)")[:, 0:w]

        @block.sync
        def _(sp):
            for row, src in ((0, b_ada), (48, g_norm_mix), (56, g_norm_ffn), (64, g_final),
                             (72, g_attn_out), (78, g_conv_out), (80, conv_w)):
                flat = src if len(src.shape) == 1 else src.rearrange(
                    "a b -> (a b)" if len(src.shape) == 2 else "a b c -> (a b c)") \
                    if len(src.shape) < 4 else src
                n = flat.shape[0] // P
                sp.dma_start(vrows[row:row + n, :], flat.rearrange("(r c) -> r c", c=P)).then_inc(in_rows, 16)
            sp.dma_start(crow[0:1, :], c_prompt).then_inc(in_rows, 16)
            sp.dma_start(crow[1:9, :], c_sample).then_inc(in_rows, 16)
            sp.dma_start(srows[0:2 * NSEQ, :], state_conv.rearrange("l b j c -> (l b j) c")).then_inc(in_rows, 16)
            sp.dma_start(ident[:, :], c_ident).then_inc(in_rows, 16)
            sp.dma_start(xtok[:, 0:2, :], x_prompt.rearrange("b (t p) d -> p (b t) d", p=P)).then_inc(in_x, 16)
            sp.dma_start(xtok[0:NSAMP, 2, :], x_sample.rearrange("b t d -> (b t) d")).then_inc(in_x, 16)

            def col_piece(n, w, c):
                sp.dma_start(slot_w(n), w[:, c * 256:(c + 1) * 256].rearrange("(k p) c -> p k c", p=P)) \
                    .then_inc(piece_in[n % SLOTS], 16)

            def free(n):
                if n >= SLOTS:
                    sp.wait_ge(pieces_used, n - SLOTS + 1)

            def load_k(s, chunks=range(CHUNKS)):
                for c in chunks:
                    if (not isinstance(s, int) or s > 0) and c < RECENT:
                        sp.wait_ge(k_used, (s - 1) * CHUNKS + c + 1)
                    sp.dma_start(K[:, c, :], key_rows(cache_k, s, c)).then_inc(k_in[c], 16)

            def load_v(s, s_keys=None):
                if not isinstance(s, int) or s > 0:
                    sp.wait_ge(v_used, s)
                for c in range(CHUNKS):
                    if c == RECENT - 1 and s_keys is not None:
                        sp.wait_ge(k_used, s_keys * CHUNKS)
                    sp.dma_start(V[:, c, :], key_rows(cache_v, s, c)).then_inc(v_in, 16)

            def key_rows(cache, s, c):
                a = cache[0, ds(s, 1), :, :, :].rearrange("o r h e -> (o r) (h e)")
                if c < RECENT:
                    return a[PAST - 512 + c * P:PAST - 512 + (c + 1) * P, :]
                g0 = (c - RECENT) * 32
                return a[g0 * 16:(g0 + 32) * 16, :].rearrange("(g r) f -> g r f", r=16)[:, 0:4, :]

            def ada_piece(n, i):
                free(n)
                r, c = (i % KD) * P, (i // KD) * ADA_COLS
                sp.dma_start(ring[:, n % SLOTS, :], w_ada[0, r:r + P, c:c + ADA_COLS]).then_inc(piece_in[n % SLOTS], 16)

            for i in range(KD):
                ada_piece(i, i)
            for dst, src in ((rope[:, :, :, :], c_rope), (lcp[:, :], c_lcp), (lcs[:, :], c_lcs), (lcn[:, :, :], c_lcn)):
                sp.dma_start(dst, src).then_inc(in_tab, 16)
            for c in range(IN_PIECES):
                free(IN0 + c)
                col_piece(IN0 + c, w_in[0], c)
            sp.wait_ge(h_ready, KD)
            load_k(0)
            for i in range(KD, KD + SLOTS):
                ada_piece(ADA0 + i - KD, i)
            sp.wait_ge(rope_done, 6)
            load_v(0)
            for i in range(KD + SLOTS, ADA_PIECES):
                ada_piece(ADA0 + i - KD, i)
            for c in range(OUT_PIECES):
                free(OUT0 + c)
                col_piece(OUT0 + c, w_out[0], c)

            def expert_piece(e, j):
                if isinstance(e, int):
                    sp.wait_ge(pieces_used, FRONT_PIECES - SLOTS + 1 + j)
                else:
                    if j % 4 == 3:
                        sp.wait_ge((gate_made, up_made, down_made)[j // 4], UNITS * e)
                    else:
                        sp.wait_ge(weights_used, 9 * (e - 1) + 3 * (j // 4) + j % 4 + 1)
                r = (j % 4) * 256
                src = (w_gate, w_up, w_down)[j // 4][0, ds(e, 1), r:r + 256, :]
                sp.dma_start(slot_w(moe_slot(j), rows=True), src.rearrange("o (k p) c -> p (o k) c", p=P)) \
                    .then_inc(piece_in[moe_slot(j)], 16)

            for j in range(EARLY):
                expert_piece(0, j)
            load_k(1, range(0, RECENT))
            sp.wait_ge(k_used, CHUNKS)
            load_k(1, range(RECENT, CHUNKS))
            with sp.Fori(2, NSEQ) as s:
                load_k(s, range(0, RECENT))
                load_v(s - 1, s)
                load_k(s, range(RECENT, CHUNKS))
            load_v(NSEQ - 1)
            for j in range(EARLY, EXP_PIECES):
                expert_piece(0, j)
            with sp.Fori(1, NEXP) as e:
                for j in range(EXP_PIECES):
                    expert_piece(e, j)

        @block.gpsimd
        def _(pool):
            pool.wait_ge(rope_done, 6)
            pool.wait_ge(z_copied, 54)
            zk, zv = Z[:, :, ATT:2 * ATT], Z[:, :, 2 * ATT:3 * ATT]
            pool.dma_start(k_prompt.rearrange("l b (t p) h e -> p (l b t) (h e)", p=P), zk[:, 0:2, :]).then_inc(k_stored, 16)
            pool.dma_start(k_sample.rearrange("l b t h e -> (l b t) (h e)"), zk[0:NSAMP, 2, :]).then_inc(k_stored, 16)
            pool.dma_start(v_prompt.rearrange("l b (t p) h e -> p (l b t) (h e)", p=P), zv[:, 0:2, :]).then_inc(out_kv, 16)
            pool.dma_start(v_sample.rearrange("l b t h e -> (l b t) (h e)"), zv[0:NSAMP, 2, :]).then_inc(out_kv, 16)
            pool.wait_ge(conv_rows, 1)
            pool.dma_start(conv_prompt.rearrange("l b j c -> (l b j) c"), COT[0:2, :]).then_inc(conv_stored, 16)
            pool.dma_start(conv_sample.rearrange("l b j c -> (l b j) c"), COT[2:NCS, :]).then_inc(conv_stored, 16)
            pool.wait_ge(k_stored, 16 * 2)
            pool.wait_ge(out_kv, 16 * 2)
            pool.wait_ge(conv_stored, 16 * 2)
            pool.wait_ge(o_copied, 2 * HPS * NSEQ)
            for dst, src in ((brow[0][0:NEXP, :], b_gate[0]), (brow[1][0:NEXP, :], b_up[0]),
                             (brow[2][0:NEXP, :], b_down[0]),
                             (wr, w_router[0].rearrange("(k p) e -> p k e", p=P)),
                             (brrow[0:1, :], b_router), (iota, c_iota), (tri, c_tri)):
                pool.dma_start(dst, src).then_inc(in_moe, 16)
            for t, (t0, tn) in enumerate(TOK_TILES):
                pool.wait_ge(y_copied, 3 + t + 1)
                dst = y_prompt[0, t0:t0 + P, :] if t < 2 else y_sample.rearrange("b t d -> (b t) d")
                pool.dma_start(dst, ytok[0:tn, t, :]).then_inc(out_end, 16)
            pool.wait_ge(out_end, 16 * 3)

        @block.tensor
        def _(te):
            tr = te.transpose

            def take_wait():
                te.sem_inc(pe_passed, 1)

            def mm(out, a, b, first, last):
                return te.matmul(out, a, b, start=first, stop=last)

            te.wait_ge(in_rows, 16 * 11)
            te.wait_ge(in_x, 32)
            tr(ps[:, 0, 0:86], vrows[0:86, :], ident[0:86, 0:86])
            for c in range(KC):
                last = tr(ps[:, 0, 96 + 16 * c:112 + 16 * c], srows[0:16, c * P:(c + 1) * P], ident[0:16, 0:16])
            step(last, vec_T)
            for k in range(KD):
                if k == KD - 1:
                    te.wait_ge(vec_copied, 1)
                b = (k + 1) % 8
                for t, (t0, tn) in enumerate(TOK_TILES):
                    last = tr(ps[:, b, t0:t0 + tn], xtok[0:tn, t, k * P:(k + 1) * P], ident[0:tn, 0:tn])
                step(last, x_T)
            te.wait_ge(silu, 1)
            te.wait_ge(x_copied, 1 + 0)
            for k in range(KD):
                last = tr(ps[:, 1, 16 * k:16 * k + 9], crow[0:9, k * P:(k + 1) * P], ident[0:9, 0:9])
            step(last, c_T)

            def sumsq(src, ks, b, name, squared, before=0):
                for i, k in enumerate(ks):
                    te.wait_ge(squared, before + i // 2 + 1)
                    last = mm(ps[:, b, 0:NT], ones[:, :], src[:, k, :], k == ks[0], k == ks[-1])
                step(last, name)

            sumsq(scratch, range(KD), 2, x_ss, x_sq)
            def modulations(n, k, b):
                arrived(te, n)
                for j in range(4):
                    last = mm(ps[32 * j:32 * j + 32, b, :], cT[:, k, :], ring[:, n % SLOTS, j * 512:(j + 1) * 512],
                              k == 0, k == KD - 1)
                last.then_inc(pieces_used, 1)

            def modulations_T(b, i):
                te.wait_ge(mods_copied, i + 1)
                for c in range(4):
                    last = tr(ps[:, b, c * P:(c + 1) * P], mod_rows[:, c * P:(c + 1) * P], ident[:, :])
                step(last, mods_T)

            te.wait_ge(c_copied, 1)
            te.wait_ge(x_copied, 1 + 7)
            for k in range(KD):
                modulations(k, k, 0)
            modulations_T(0, 0)
            for c in range(9):
                n = IN0 + c
                arrived(te, n)
                w = slot_w(n)
                for t, (t0, tn) in enumerate(TOK_TILES):
                    b = 1 + (3 * c + t) % 6
                    if c >= 2:
                        te.wait_ge(z_copied, 6 * (c - 2) + (1, 2, 6)[t])
                    for k in range(KD):
                        if c == 0 and t == 0:
                            te.wait_ge(h_ready, k + 1)
                        if t < 2:
                            last = mm(ps[:, b, 0:256], hT[:, k, t0:t0 + tn], w[:, k, :], k == 0, k == KD - 1)
                        else:
                            for j in range(4):
                                last = mm(ps[32 * j:32 * j + 32, b, 0:64], hT[:, k, t0:t0 + tn],
                                          w[:, k, 64 * j:64 * j + 64], k == 0, k == KD - 1)
                    if t < 2:
                        step(last, z_made)
                last.then_inc(pieces_used, 1)
            for c in range(3):
                n = IN0 + 9 + c
                arrived(te, n)
                w = slot_w(n)
                for j in range(2):
                    b = 1 + (2 * c + j) % 6
                    te.wait_ge(z_copied, 54 if 2 * c + j < 3 else 48)
                    for k in range(KD):
                        last = mm(ps[:, b, 0:NT], w[:, k, j * P:(j + 1) * P], hT[:, k, :], k == 0, k == KD - 1)
                    if j == 0:
                        step(last, bcu_made)
                last.then_inc(pieces_used, 1)
            te.wait_ge(rope_done, 6)
            for i in range(2 * PAIRS):
                last = tr(ps[:, 0, 32 * i:32 * i + 32], Z[0:NSAMP, 2, i * P:(i + 1) * P], ident[0:32, 0:32])
            step(last, qk_samp_T)
            for hp in range(PAIRS):
                b = 7 if hp % 2 == 0 else 0
                if hp == 1:
                    te.wait_ge(q_blocks_set, 1)
                if hp >= 2:
                    te.wait_ge(qk_copied, hp - 2 + 1)
                for i in range(4):
                    src = Z[:, i % 2, (i // 2) * ATT + hp * P:(i // 2) * ATT + (hp + 1) * P]
                    last = tr(ps[:, b, i * P:(i + 1) * P], src, ident[:, :])
                step(last, qk_T)
            te.wait_ge(conv_last, 1)
            te.wait_ge(qk_copied, PAIRS - 1 + 1)
            for c in range(KC):
                last = tr(ps[0:NCS, 0, c * P:(c + 1) * P], CO[:, c, :], ident[:, :])
            step(last, conv_rows_T)

            def p_scores(h):
                hp, a = h // 2, HD * (h % 2)
                if h >= 2:
                    te.wait_ge(p_masked, h - 2 + 1)
                qT = Z[a:a + HD, 0:2, hp * P:(hp + 1) * P]
                kT = Z[a:a + HD, 0:2, ATT + hp * P:ATT + (hp + 1) * P]
                mm(ps[:, 1 + h % 2, 0:128], qT[:, 0, :], kT[:, 0, :], True, True)
                step(mm(ps[:, 1 + h % 2, 128:384].rearrange("p (t k) -> p t k", t=2), qT[:, 1, :], kT,
                           True, True), p_scores_made)

            def p_values(h):
                a = HD * (h % 2)
                te.wait_ge(p_T_copied, h + 1)
                if h >= 2:
                    te.wait_ge(p_out_copied, h - 2 + 1)
                ob = 5 + h % 2
                v0 = 2 * ATT + h * HD
                mm(ps[a:a + HD, ob, 0:P], Z[:, 0, v0:v0 + HD], pPT[h % 2][:, 0:P], True, True)
                for i in range(2):
                    last = mm(ps[a:a + HD, ob, P:2 * P], Z[:, i, v0:v0 + HD],
                              pPT[h % 2][:, (1 + i) * P:(2 + i) * P], i == 0, i == 1)
                step(last, p_out_made)

            te.wait_ge(bcu_copied, 6)
            te.wait_ge(conv_done, 1)
            p_scores(0)
            p_scores(1)
            for h in range(HEADS):
                if h + 2 < HEADS:
                    p_scores(h + 2)
                if h == 0:
                    te.wait_ge(conv_rows, 1)
                for i in range((ADA_PIECES - KD) * h // HEADS, (ADA_PIECES - KD) * (h + 1) // HEADS):
                    modulations(ADA0 + i, i % KD, (7, 0)[i // KD])
                te.wait_ge(p_normed, 2 * (h) + 2)
                if h >= 2:
                    te.wait_ge(p_T_copied, h - 2 + 1)
                for i in range(3):
                    last = tr(ps[:, 3 + h % 2, i * P:(i + 1) * P], pP[h % 3][:, i * P:(i + 1) * P], ident[:, :])
                step(last, p_T)
                if h >= 1:
                    p_values(h - 1)
            p_values(HEADS - 1)

            modulations_T(7, 1)
            modulations_T(0, 2)
            te.wait_ge(p_out_copied, HEADS)
            te.wait_ge(mods_ready, 3)

            def keys_T(s, c):
                te.wait_ge(k_in[c], 16 * (s + 1))
                if c >= 2:
                    te.wait_ge(kt_copied_a, CHUNKS * s + c - 1)
                    if c >= 4:
                        te.wait_ge(kt_copied_d, HALF_D * s + c - 3)
                elif not isinstance(s, int) or s > 0:
                    te.wait_ge(kt_copied_a, CHUNKS * s)
                    te.wait_ge(kt_copied_d, HALF_D * s)
                b = 2 * (c % 2)
                for hp in range(PAIRS):
                    last = tr(ps[:, b + hp // 4, (hp % 4) * P:(hp % 4 + 1) * P], K[:, c, hp * P:(hp + 1) * P], ident[:, :])
                last.then_inc(k_used, 1)

            def scores_of(out, keys):
                for o in range(2):
                    for j in range(SETS):
                        half, jp = divmod(j, 2)
                        last = mm(out(j), qb[:, 2 * j + o, :], keys(3 * half + jp + o), o == 0, o == 1)
                return last

            def scores(s, c):
                te.wait_ge(kt_copied_a, CHUNKS * s + c + 1)
                if c >= 2:
                    te.wait_ge(kt_copied_d, HALF_D * s + c - 1)
                if c == 0:
                    te.wait_ge(qb_ready, s + 1)
                    if not isinstance(s, int) or s > 0:
                        te.wait_ge(s_masked, 3 * s - 2)
                    take_wait()
                if c == 4 and (not isinstance(s, int) or s > 0):
                    te.wait_ge(s_masked, 3 * s)
                    take_wait()
                b, c0 = 5 + c // 4, (c % 4) * P
                scores_of(lambda j: ps[32 * j:32 * j + 32, b, c0:c0 + P],
                          lambda hp: KT[c % 2][:, hp, :]).then_inc(st_made, 1)

            def scores_new():
                scores_of(lambda j: ps[32 * j:32 * j + 32, 6, 384:384 + NSAMP],
                          lambda hp: kTs[:, hp, :]).then_inc(s_made, 1)

            def probs_T(s):
                te.wait_ge(s_exp, s + 1)
                if not isinstance(s, int) or s > 0:
                    te.wait_ge(o_copied, 2 * HPS * s)
                take_wait()
                for c in range(CHUNKS):
                    tr(ps[:, 4 + 3 * (c // 4), (c % 4) * P:(c % 4 + 1) * P], sP[:, c * P:(c + 1) * P], ident[:, :])
                tr(ps[0:NSAMP, 7, 384:512], sP[:, KEYS:KEYS + NSAMP], ident[:, :]).then_inc(pt_made, 1)

            def values(s):
                te.wait_ge(v_in, 16 * CHUNKS * (s + 1))
                te.wait_ge(pt_copied, 3 * s + 3)
                take_wait()
                w = HPS * HD
                for c in range(CHUNKS):
                    for j in range(SETS):
                        mm(ps[32 * j:32 * j + 32, 4, 0:w], PT[:, c, 32 * j:32 * j + 32],
                           V[:, c, w * j:w * j + w], c == 0, False)
                for j in range(SETS):
                    last = mm(ps[32 * j:32 * j + 32, 4, 0:w], PT[0:NSAMP, CHUNKS, 32 * j:32 * j + 32],
                              Z[0:NSAMP, 2, 2 * ATT + w * j:2 * ATT + w * j + w], False, True)
                last.then_inc(v_used, 1)

            def outputs_T(s):
                te.wait_ge(o_scaled, s + 1)
                take_wait()
                for i in range(HPS):
                    for a in range(2):
                        last = mm(ps[a * HD:(a + 1) * HD, 7, i * P:(i + 1) * P], o_sb[:, i * HD:(i + 1) * HD],
                                  ident[:, :], True, True)
                last.then_inc(o_T, 1)

            for c in range(CHUNKS):
                keys_T(0, c)
                if c >= 1:
                    scores(0, c - 1)
            scores(0, CHUNKS - 1)
            scores_new()

            def sequence(s):
                for c in range(CHUNKS):
                    keys_T(s + 1, c)
                    if c >= 1:
                        scores(s + 1, c - 1)
                    if c == 3:
                        probs_T(s)
                    if c == 4:
                        values(s)
                scores(s + 1, CHUNKS - 1)
                scores_new()
                outputs_T(s)

            sequence(0)
            with te.Fori(1, NSEQ - 1) as s:
                sequence(s)
            probs_T(NSEQ - 1)
            values(NSEQ - 1)
            outputs_T(NSEQ - 1)

            sumsq(scratch, range(KA, KD), 1, conv_ss, cat_sq)
            sumsq(scratch, range(KA), 0, att_ss, cat_sq, 1)
            for c in range(KD):
                n = OUT0 + c // 2
                arrived(te, n)
                w = slot_w(n)
                b = 2 + c % 6
                if c >= 6:
                    te.wait_ge(x1_ready, c - 6 + 1)
                for k in range(KD):
                    if c == 0:
                        te.wait_ge(cat_ready, k + 1)
                    last = mm(ps[:, b, 0:NT], w[:, k, (c % 2) * P:(c % 2 + 1) * P], hT[:, k, :], k == 0, k == KD - 1)
                last.then_inc(pieces_used if c % 2 else mix_made, 1)
            te.wait_ge(in_moe, 16 * 7)
            for j in range(2):
                for k in range(KD):
                    last = tr(ps[:, 0, j * 256 + k * 32:j * 256 + (k + 1) * 32], brow[j][0:NEXP, k * P:(k + 1) * P],
                              ident[0:NEXP, 0:NEXP])
            step(last, bias_T)
            sumsq(scratch, range(KD), 1, x1_ss, x1_sq)
            for k in range(KD):
                te.wait_ge(h2_ready, k + 1)
                last = mm(ps[0:NEXP, 2, 0:NT], wr[:, k, :], hT[:, k, :], k == 0, k == KD - 1)
            step(last, logits_T)
            te.wait_ge(logits_copied, 1)
            for t, (t0, tn) in enumerate(TOK_TILES):
                mm(ps[0:tn, 2, t * 32:(t + 1) * 32], GT[0:NEXP, t0:t0 + tn], ident[0:NEXP, 0:NEXP], True, False)
                last = mm(ps[0:tn, 2, t * 32:(t + 1) * 32], ones[0:1, 0:tn], brrow[0:1, :], False, True)
            step(last, logits_made)
            for t, (t0, tn) in enumerate(TOK_TILES):
                for j in range(2):
                    b = 3 + (2 * t + j) % 4
                    if t == 2:
                        te.wait_ge(h2_copied, j + 1)
                    for k in range(4):
                        last = tr(ps[0:tn, b, k * P:(k + 1) * P], hT[:, 4 * j + k, t0:t0 + tn], ident[:, :])
                    step(last, h2_T)
            te.wait_ge(selected, 1)
            for t, (t0, tn) in enumerate(TOK_TILES):
                for u in range(t):
                    mm(ps[0:tn, 7, t * 32:(t + 1) * 32], ones[:, 0:tn], sel[:, u, :], u == 0, False)
                mm(ps[0:tn, 7, t * 32:(t + 1) * 32], tri[0:tn, 0:tn], sel[0:tn, t, :], t == 0, True)
            for t, (t0, tn) in enumerate(TOK_TILES):
                mm(ps[0:1, 7, 96:128], ones[0:tn, 0:1], sel[0:tn, t, :], t == 0, t == 2)
            for t, (t0, tn) in enumerate(TOK_TILES):
                last = tr(ps[0:NEXP, 1, t0:t0 + tn], G[0:tn, t, :], ident[0:tn, 0:tn])
            step(last, places_made)
            te.wait_ge(h2_copied, 6)
            te.wait_ge(counts_ready, 1)

            def count(e):
                a = cnt[0:1, e:e + 1] if isinstance(e, int) else cnt[0:1, ds(e, 1)]
                return te.value_load(a.bitcast(I32), min_val=0, max_val=NT)

            def gather(e, N):
                n = gather_width(N)
                per = gather_chunks(n)
                hot = Poh[:, 0:3 * n].rearrange("p (t n) -> p t n", n=n)
                te.wait_ge(onehot, e + 1)
                for g in range(0, KD, per):
                    i = g // per
                    if i >= 2:
                        te.wait_ge(xe_ready, KD * e + g - per)
                    for k in range(g, g + per):
                        out = ps[:, 6 + i % 2, (k - g) * n:(k - g + 1) * n]
                        for t in range(3):
                            last = mm(out, h2tok[:, t, k * P:(k + 1) * P], hot[:, t, :], t == 0, t == 2)
                    last.then_inc(gathered, per)

            def tokens_by_weights(e, x, pieces, b, m, wait_pieces, done_pieces, made, by, wait_x=None):
                w = KD * m
                for k in range(KD):
                    j = pieces[k // 2]
                    if wait_x:
                        wait_x(k)
                    if wait_pieces and k % 2 == 0:
                        te.wait_ge(piece_in[moe_slot(j)], 16 * ((FRONT_PIECES + j) // SLOTS + 1) + 16 * e)
                    W = slot_w(moe_slot(j), rows=True)
                    for half in range(parts(m)):
                        wc = min(w, 512)
                        for q in range(P // m):
                            c0 = q * w + half * 512
                            last = mm(ps[q * m:(q + 1) * m, b + half, 0:wc], x(k), W[:, k % 2, c0:c0 + wc],
                                      k == 0, k == KD - 1)
                    if done_pieces and k % 2 == 1 and k < KD - 1:
                        last.then_inc(weights_used, 1)
                last.then_inc(made, by)

            def rows_T(e, N, i):
                m = slot_tiles(N)[i][1]
                by = unit(N) // parts(m)
                done = UNITS * e + unit(N) * (i + 1)
                te.wait_ge(gate_copied, done)
                te.wait_ge(up_copied, done)
                if 0 < i < len(slot_tiles(N)) - 1:
                    te.wait_ge(g_biased, done - unit(N))
                    te.wait_ge(u_biased, done - unit(N))
                if i == 0 and len(slot_tiles(N)) > 1:
                    te.wait_ge(acc_ready, KD * e + KD)
                bg, bu = rows_T_banks(N, i)
                for p in range(parts(m)):
                    for src, b, made in ((gate_rows, bg, gate_T), (up_rows, bu, up_T)):
                        for c in range(min(4, KD * m // P)):
                            last = tr(ps[:, b + p, c * P:(c + 1) * P], src[:, p * 512 + c * P:p * 512 + (c + 1) * P],
                                      ident[:, :])
                        last.then_inc(made, by)

            def gate_up(e, N, first):
                xs = xe[:, 0:KD * gather_width(N)].rearrange("p (k n) -> p k n", k=KD)
                te.wait_ge(xe_ready, KD * e + KD)
                for i, (s0, m) in enumerate(slot_tiles(N)):
                    if i >= first:
                        tokens_by_weights(e, lambda k: xs[:, k, s0:s0 + m], GATE, 0, m, i == 0, s0 + m == N, gate_made, unit(N))
                    if i == 0 and first == 0:
                        return
                    tokens_by_weights(e, lambda k: xs[:, k, s0:s0 + m], UP, 2, m, i == 0, s0 + m == N, up_made, unit(N))
                    if i < len(slot_tiles(N)) - 1:
                        rows_T(e, N, i)

            def hot_T(e, N):
                tiles = slot_tiles(N)
                te.wait_ge(acc_ready, KD * e + KD)
                if len(tiles) > 1:
                    te.wait_ge(g_biased, UNITS * e + unit(N) * (len(tiles) - 1))
                    te.wait_ge(u_biased, UNITS * e + unit(N) * (len(tiles) - 1))
                for i in range(len(tiles)):
                    te.wait_ge(onehot_g, UNITS * e + unit(N) * (i + 1))
                    if i == 2:
                        te.wait_ge(hot_T_ready, UNITS * e + unit(N))
                    for t, (t0, tn) in enumerate(TOK_TILES):
                        last = tr(ps[:, 4 + i % 2, t0:t0 + tn], Pg[0:tn, t, i * P:(i + 1) * P], ident[0:tn, 0:tn])
                    last.then_inc(hot_T_made, unit(N))

            def down(e, N):
                for i, (s0, m) in enumerate(slot_tiles(N)):
                    if i == 0:
                        te.wait_ge(hot_T_ready, UNITS * e + UNITS)
                    nq = P // m
                    done = UNITS * e + unit(N) * i
                    if i or not isinstance(e, int) or e > 0:
                        te.wait_ge(ye_ready, done)
                    def x(k):
                        q, c = divmod(k, KD // nq)
                        a = KD * s0 + (c * nq + q) * m
                        return actT[:, a:a + m]
                    def wait_x(k):
                        if k % (KD // parts(m)) == 0:
                            te.wait_ge(act_ready, done + unit(N) // parts(m) * (k // 4 + 1))
                    tokens_by_weights(e, x, DOWN, 4, m, i == 0, s0 + m == N, down_made, unit(N), wait_x)

            def combine(e, N):
                te.wait_ge(ye_ready, UNITS * e + UNITS)
                te.wait_ge(hot_T_ready, UNITS * e + UNITS)
                tiles = slot_tiles(N)
                for c in range(KD):
                    if c >= 4 and c % 2 == 0:
                        te.wait_ge(acc_ready, KD * (e + 1) + c - 2)
                    for i, (s0, m) in enumerate(tiles):
                        q, cc = divmod(c, KD * m // P)
                        last = mm(ps[:, comb_bank(c), 0:NT], ye[:, i, cc * P:(cc + 1) * P], bd_tile(m, i)[:, q, :],
                                  i == 0, i == len(tiles) - 1)
                    last.then_inc(comb_made, 1)

            by_width(te, count(0), lambda N: gather(0, N))

            def start_acc():
                te.wait_ge(bias_copied, 1)
                te.wait_ge(gates_T, 1)
                for c in range(KD):
                    if c >= 4:
                        te.wait_ge(acc_ready, c - 3)
                    step(mm(ps[:, comb_bank(c), 0:NT], brow[2][0:NEXP, c * P:(c + 1) * P], GT[0:NEXP, :], True, True), acc0_made)

            def expert(e, first, last):
                n = count(e)
                by_width(te, n, lambda N: gate_up(e, N, 0))
                if first:
                    start_acc()
                else:
                    n0 = count(e - 1)
                    by_width(te, n0, lambda N: combine(e - 1, N))
                by_width(te, n, lambda N: (gate_up(e, N, 1), hot_T(e, N), rows_T(e, N, len(slot_tiles(N)) - 1)))
                if not last:
                    n1 = count(e + 1)
                    by_width(te, n1, lambda N: gather(e + 1, N))
                by_width(te, n, lambda N: down(e, N))

            expert(0, True, False)
            with te.Fori(1, NEXP - 1) as e:
                expert(e, False, False)
            expert(NEXP - 1, False, True)
            by_width(te, count(NEXP - 1), lambda N: combine(NEXP - 1, N))

            sumsq(scratch, range(KD), 0, x2_ss, x2_sq)
            for j in range(2):
                te.wait_ge(y_ready, 4 * j + 4)
                for t, (t0, tn) in enumerate(TOK_TILES):
                    for k in range(4):
                        last = tr(ps[0:tn, 1 + 2 * t + j, k * P:(k + 1) * P], hT[:, 4 * j + k, t0:t0 + tn], ident[:, :])
                    step(last, y_T)
            

        @block.vector
        def _(ve):

            def go(ins, signal=dve_step):
                ve.wait_ge(signal, step(ins, signal))

            def TT(out, a, b, op):
                return ve.tensor_tensor(out, a, b, op)

            go(ve.memset(ones[:, :], 1.0))
            go(ve.memset(cT[:, :, :], 0.0), cT_zero)
            go(ve.memset(eps[:, :], EPS), ones_set)
            ve.wait_ge(vec_T, 1)
            go(ve.tensor_copy(vec[:, :], ps[:, 0, 0:86]))
            ces = CES.rearrange("p c (s j) -> p c s j", j=6)
            go(ve.tensor_copy(cst[:, :], ps[:, 0, 96:128]), vec_copied)
            ve.wait_ge(c_sig, 1)
            go(TT(crow[0:9, :], crow[0:9, :], csig[0:9, :], ALU.mult), silu)
            ve.wait_ge(c_T, 1)
            go(ve.tensor_copy(cT[:, :, 0:9], ps[:, 1, 0:128].rearrange("p (k c) -> p k c", c=16)[:, :, 0:9]), c_copied)

            def recip(r, std):
                ve.wait_ge(std, 1)
                go(ve.reciprocal(r, r))

            def bc_k(r, n=KD):
                return r.unsqueeze(1).to_broadcast([P, n, NT])

            recip(rstd, x_std)
            ve.wait_ge(x_copied, 1 + 7)
            go(TT(hT[:, :, :], xT[:, :, :], bc_k(rstd), ALU.mult))

            def modulations(b, i):
                ve.wait_ge(mods_T, i + 1)
                f = slice(2 * KD * i, 2 * KD * (i + 1))
                go(TT(mods[:, f, :].rearrange("p (j c) s -> p c j s", j=4),
                      ps[:, b, :].rearrange("p (c j s) -> p c j s", c=4, j=4)[:, :, :, 0:9],
                      vec[:, f].rearrange("p (j c) -> p c j", j=4).unsqueeze(3).to_broadcast([P, 4, 4, 9]), ALU.add),
                   mods_ready)

            def one_plus_scale(gs, g, f):
                go(ve.scalar_tensor_tensor(gs[:, :, :], mods[:, f:f + 8, :], 1.0,
                                           g.unsqueeze(2).to_broadcast([P, KD, 9]), ALU.add, ALU.mult))

            modulations(0, 0)
            one_plus_scale(gs1, g_mix, 8)

            def samp(t):
                return t[:, :, SEQ:NT].rearrange("p k (s t) -> p k s t", t=TS)

            def per_seq(m):
                return m.unsqueeze(3).to_broadcast([P, KD, NSEQ, TS])

            def modulate_samples(gs, f, name):
                go(TT(samp(hT), samp(hT), per_seq(gs[:, :, 1:9]), ALU.mult))
                go(TT(samp(hT), samp(hT), per_seq(mods[:, f:f + 8, 1:9]), ALU.add), name)

            modulate_samples(gs1, 0, dve_step)
            for k in range(KD):
                step(ve.tensor_scalar(hT[:, k, 0:SEQ], hT[:, k, 0:SEQ], gs1[:, k, 0:1], mods[:, k, 0:1],
                                      ALU.mult, ALU.add), h_ready)

            ve.wait_ge(in_tab, 16 * 4)
            for part in range(2):
                ve.wait_ge(z_copied, 6 * (3 * part + 2) + 6)
                for t, (t0, tn) in enumerate(TOK_TILES):
                    x = Z[0:tn, t, part * ATT:(part + 1) * ATT].rearrange("p (h e) -> p h e", e=HD)
                    r1 = rope1[0:tn, :].rearrange("p (h e) -> p h e", e=HD)
                    r2 = rope2[0:tn, :].rearrange("p (h e) -> p h e", e=HD)
                    H = HD // 2

                    def table(i, e0, n):
                        return rope[0:tn, t, i, e0:e0 + n].unsqueeze(1).to_broadcast([tn, HEADS, n])

                    go(TT(r1, x, table(0, 0, HD), ALU.mult))
                    go(TT(r2[:, :, 0:H], x[:, :, H:HD], table(1, 0, H), ALU.mult))
                    go(TT(r2[:, :, H:HD], x[:, :, 0:H], table(1, H, H), ALU.mult))
                    go(TT(x, r1, r2, ALU.add), rope_done)

            ve.wait_ge(qk_samp_T, 1)
            go(ve.tensor_copy(qTs[:, :, :], ps[:, 0, 0:192].rearrange("p (h n) -> p h n", h=PAIRS)))
            go(ve.tensor_copy(kTs[:, :, :], ps[:, 0, 192:384].rearrange("p (h n) -> p h n", h=PAIRS)), q_blocks_set)

            ve.wait_ge(bcu_copied, 6)
            go(ve.tensor_copy(ces[:, :, :, 0:2], cst[:, :].rearrange("p (c s j) -> p c s j", c=KC, j=2)))
            go(TT(ces[:, :, :, 2:6], samp(BCU[:, 2:4, :]), samp(BCU[:, 4:6, :]), ALU.mult))
            go(TT(BCU[:, 4:6, 0:SEQ], BCU[:, 2:4, 0:SEQ], BCU[:, 4:6, 0:SEQ], ALU.mult))
            go(ve.tensor_copy(CO[:, :, 0:2], BCU[:, 4:6, SEQ - 2:SEQ]))
            go(ve.tensor_copy(CO[:, :, 2:NCS].rearrange("p c (s j) -> p c s j", j=2), ces[:, :, :, 4:6]), conv_last)
            for c in range(KC):
                w = [taps[:, KC * j + c:KC * j + c + 1] for j in range(3)]
                y, cu = hT[:, KA + c, 0:SEQ], BCU[:, 4 + c, 0:SEQ]
                go(ve.tensor_scalar(y, cu, w[2], None, ALU.mult))
                for j in (1, 0):
                    d = 2 - j
                    go(ve.scalar_tensor_tensor(y[:, d:SEQ], cu[:, 0:SEQ - d], w[j], y[:, d:SEQ], ALU.mult, ALU.add))
                y = hT[:, KA + c, SEQ:NT].rearrange("p (s t) -> p s t", t=TS)
                go(ve.tensor_scalar(y, ces[:, c, :, 2:6], w[2], None, ALU.mult))
                for j in (1, 0):
                    go(ve.scalar_tensor_tensor(y, ces[:, c, :, j:j + 4], w[j], y, ALU.mult, ALU.add))
            go(TT(hT[:, KA:KD, :], hT[:, KA:KD, :], BCU[:, 0:2, :], ALU.mult), conv_done)

            blocks = ((0, 128), (128, 256))
            def p_mask(h):
                b = pP[h % 3]
                ve.wait_ge(p_scores_made, h + 1)
                if h >= 3:
                    ve.wait_ge(p_T, h - 3 + 1)
                go(ve.scalar_tensor_tensor(b, ps[:, 1 + h % 2, 0:384], SCALE, lcp[:, :], ALU.mult, ALU.add), p_masked)
                for i, (c0, cn) in enumerate(blocks):
                    go(ve.tensor_reduce(stat[:, 4 * (h % 3) + i:4 * (h % 3) + i + 1], b[:, c0:c0 + cn], AX.X, ALU.max,
                                        negate=True), p_max)

            def p_norm(h):
                b, s = pP[h % 3], stat[:, 4 * (h % 3) + 2:4 * (h % 3) + 4]
                ve.wait_ge(p_exped, 2 * (h) + 2)
                go(ve.reciprocal(s, s))
                for i, (c0, cn) in enumerate(blocks):
                    go(ve.tensor_scalar(b[:, c0:c0 + cn], b[:, c0:c0 + cn], s[:, i:i + 1], None, ALU.mult), p_normed)

            p_mask(0)
            p_mask(1)
            for h in range(HEADS):
                p_norm(h)
                if h + 2 < HEADS:
                    p_mask(h + 2)

            modulations(7, 1)
            modulations(0, 2)
            one_plus_scale(gs2, g_ffn, 32)

            ve.wait_ge(p_out_made, HEADS - 1 + 1)

            go(ve.memset(qb, 0.0), qb_zero)
            go(ve.memset(qb_all, 0.0), qb_zero)
            blocks_all = qb_all.rearrange("p s (b j o r) -> p s b (j o) r", b=2, j=2, o=2)
            for jp in range(2):
                for i in range(HPS):
                    lp, a = divmod(3 * jp + i, 2)
                    r = slice(a * HD, (a + 1) * HD)
                    q = qTs[r, :, :].rearrange("p (b k) (s t) -> p b k s t", b=2, t=TS)[:, :, lp, :, :]
                    step(ve.tensor_copy(blocks_all[r, :, :, 2 * jp + lp - jp, TS * i:TS * i + TS],
                                        q.rearrange("p b s t -> p s b t")), qb_made)

            def v_keys(s, c):
                ve.wait_ge(k_used, CHUNKS * s + c + 1)
                ve.tensor_copy(KT[c % 2][:, 0:4, :], ps[:, 2 * (c % 2), :].rearrange("p (h n) -> p h n", h=4)) \
                    .then_inc(kt_copied_d, 1)

            def v_mask_recent(s):
                ve.wait_ge(st_made, CHUNKS * s + 4)
                if not isinstance(s, int) or s > 0:
                    ve.wait_ge(pt_made, s)
                ve.scalar_tensor_tensor(sP[:, 0:512], ps[:, 5, :], SCALE, lcs[:, 0:512], ALU.mult, ALU.add).then_inc(s_masked, 1)
                ve.wait_ge(s_masked, 3 * s + 1)
                ve.tensor_reduce(stat[:, 12:13], sP[:, 0:512], AX.X, ALU.max, negate=True).then_inc(s_max, 1)

            def v_mask(s):
                ve.wait_ge(s_made, s + 1)
                new = lcn[:, s, :] if isinstance(s, int) else lcn[:, ds(s, 1), :].rearrange("p o n -> p (o n)")
                for dst, src, tab in ((sP[:, 512:KEYS], ps[:, 6, 0:KEYS - 512], lcs[:, 512:KEYS]),
                                      (sP[:, KEYS:KEYS + NSAMP], ps[:, 6, 384:416], new)):
                    ve.scalar_tensor_tensor(dst, src, SCALE, tab, ALU.mult, ALU.add).then_inc(s_masked, 1)
                ve.wait_ge(s_masked, 3 * s + 3)
                ve.tensor_reduce(stat[:, 13:14], sP[:, 512:KEYS + NSAMP], AX.X, ALU.max, negate=True).then_inc(s_max, 1)
                ve.wait_ge(s_max, 2 * s + 2)
                TT(stat[:, 8:9], stat[:, 12:13], stat[:, 13:14], ALU.min).then_inc(s_neg, 1)

            def v_scale(s):
                ve.wait_ge(s_exp, s + 1)
                ve.reciprocal(stat[:, 10:11], stat[:, 9:10]).then_inc(s_recip, 1)
                ve.wait_ge(s_recip, s + 1)
                ve.wait_ge(v_used, s + 1)
                ve.tensor_scalar(o_sb, ps[:, 4, 0:HPS * HD], stat[:, 10:11], None, ALU.mult).then_inc(o_scaled, 1)

            def v_outputs(s):
                ve.wait_ge(o_T, s + 1)
                n = slice(SEQ + 4 * s, SEQ + 4 * s + 4) if isinstance(s, int) else ds(4 * s + SEQ, 4)
                for jp in range(2):
                    for i in range(HPS):
                        lp, a = divmod(3 * jp + i, 2)
                        r = slice(a * HD, (a + 1) * HD)
                        src = ps[r, 7, i * P:(i + 1) * P].rearrange("p (b j r) -> p b j r", b=2, j=2)
                        dst = hT[r, 0:PAIRS, n].rearrange("p (b k) t -> p b k t", b=2)
                        ve.tensor_copy(dst[:, :, lp, :], src[:, :, jp, TS * i:TS * i + TS]).then_inc(o_copied, 1)

            for c in range(2, CHUNKS):
                v_keys(0, c)
            v_mask_recent(0)

            def sequence(s):
                v_mask(s)
                for c in range(2, CHUNKS):
                    v_keys(s + 1, c)
                    if c == 4:
                        v_scale(s)
                v_mask_recent(s + 1)
                v_outputs(s)

            sequence(0)
            with ve.Fori(1, NSEQ - 1) as s:
                sequence(s)
            v_mask(NSEQ - 1)
            v_scale(NSEQ - 1)
            v_outputs(NSEQ - 1)
            ve.wait_ge(o_copied, 2 * HPS * NSEQ)

            ve.wait_ge(out_kv, 16 * 2)
            go(ve.memset(bd_all, 0.0))
            go(ve.memset(h2tok[:, 2, :], 0.0), moe_zeros)
            recip(rstd_c, conv_std)
            recip(rstd, att_std)
            for k in range(KD):
                step(ve.scalar_tensor_tensor(hT[:, k, :], hT[:, k, :], g_cat[:, k:k + 1],
                                             rstd if k < KA else rstd_c, ALU.mult, ALU.mult), cat_ready)

            def residual(k, src, f, name):
                go(ve.scalar_tensor_tensor(xT[:, k, 0:SEQ], src[:, 0:SEQ], mods[:, f + k, 0:1], xT[:, k, 0:SEQ],
                                           ALU.mult, ALU.add))
                t = tmp32
                go(TT(t.rearrange("p (s t) -> p s t", t=TS), src[:, SEQ:NT].rearrange("p (s t) -> p s t", t=TS),
                      mods[:, f + k, 1:9].unsqueeze(2).to_broadcast([P, NSEQ, TS]), ALU.mult))
                go(TT(xT[:, k, SEQ:NT], xT[:, k, SEQ:NT], t, ALU.add), name)

            tmp32 = gs1[:, 0:4, :].rearrange("p a b -> p (a b)")[:, 0:NSAMP]
            for k in range(KD):
                if k % 2 == 0:
                    ve.wait_ge(mix_made, k // 2 + 1)
                else:
                    ve.wait_ge(pieces_used, OUT0 + k // 2 + 1)
                residual(k, ps[:, 2 + k % 6, 0:NT], 16, x1_ready)
            ve.wait_ge(bias_T, 1)
            go(ve.tensor_copy(bgT, ps[:, 0, 0:256].rearrange("p (k e) -> p k e", k=KD)))
            go(ve.tensor_copy(buT, ps[:, 0, 256:512].rearrange("p (k e) -> p k e", k=KD)), bias_copied)
            recip(rstd2, x1_std)
            go(TT(hT[:, :, SEQ:NT], xT[:, :, SEQ:NT], rstd2[:, SEQ:NT].unsqueeze(1).to_broadcast([P, KD, NSAMP]), ALU.mult))
            modulate_samples(gs2, 24, dve_step)
            for k in range(KD):
                scaled = step(ve.scalar_tensor_tensor(hT[:, k, 0:SEQ], xT[:, k, 0:SEQ], gs2[:, k, 0:1], rstd2[:, 0:SEQ],
                                                      ALU.mult, ALU.mult), h2_scaled)
                if k:
                    ve.wait_ge(h2_scaled, scaled - 1)
                    step(ve.tensor_scalar(hT[:, k - 1, 0:SEQ], hT[:, k - 1, 0:SEQ], mods[:, 24 + k - 1, 0:1], None,
                                          ALU.add), h2_ready)
            ve.wait_ge(h2_scaled, KD)
            go(ve.tensor_scalar(hT[:, KD - 1, 0:SEQ], hT[:, KD - 1, 0:SEQ], mods[:, 24 + KD - 1, 0:1], None, ALU.add), h2_ready)

            go(ve.memset(idxf, -1.0))
            go(ve.memset(gates, 0.0))
            go(ve.memset(posm, 0.0))
            ve.wait_ge(logits_made, 1)
            def tiles(op, signal=dve_step):
                for t, (t0, tn) in enumerate(TOK_TILES):
                    n = step(op(t, tn), signal)
                ve.wait_ge(signal, n)

            tiles(lambda t, tn: ve.tensor_copy(logit[0:tn, t, :], ps[0:tn, 2, t * 32:(t + 1) * 32]))
            tiles(lambda t, tn: ve.max(top8[0:tn, t, :], logit[0:tn, t, :]))
            tiles(lambda t, tn: ve.tensor_scalar(gates[0:tn, t, :], top8[0:tn, t, 0:TOPK], top8[0:tn, t, 0:1], None,
                                                 ALU.subtract), gates_less_max)
            tiles(lambda t, tn: ve.max_index(idx8[0:tn, t, :].bitcast(U32), top8[0:tn, t, :], logit[0:tn, t, :]))
            tiles(lambda t, tn: ve.tensor_copy(idxf[0:tn, t, :], idx8[0:tn, t, 0:TOPK].bitcast(U32)))
            ve.wait_ge(gates_exp, 3)
            tiles(lambda t, tn: ve.reciprocal(gsum[0:tn, t:t + 1], gsum[0:tn, t:t + 1]))
            tiles(lambda t, tn: ve.tensor_scalar(gates[0:tn, t, :], gates[0:tn, t, :], gsum[0:tn, t:t + 1], None, ALU.mult))
            e4 = eq4.rearrange("p (t j e) -> p t j e", t=3, j=TOPK)
            ie = iota[:, 0:NEXP].unsqueeze(1).unsqueeze(1).to_broadcast([P, 3, TOPK, NEXP])
            go(TT(e4, ie, idxf.unsqueeze(3).to_broadcast([P, 3, TOPK, NEXP]), ALU.is_equal))
            go(ve.tensor_reduce(sel, e4.rearrange("p t j e -> p t e j"), AX.X, ALU.add))
            go(TT(e4, e4, gates.unsqueeze(3).to_broadcast([P, 3, TOPK, NEXP]), ALU.mult))
            go(ve.tensor_reduce(G, e4.rearrange("p t j e -> p t e j"), AX.X, ALU.add), selected)
            ve.wait_ge(places_made, 1)
            for t, (t0, tn) in enumerate(TOK_TILES):
                go(ve.tensor_copy(posm[0:tn, t, :], ps[0:tn, 7, t * 32:(t + 1) * 32]))
            go(ve.tensor_copy(cnt[0:1, :].bitcast(I32), ps[0:1, 7, 96:128]))
            go(ve.scalar_tensor_tensor(posm, posm, 1.0, sel, ALU.add, ALU.mult))
            go(ve.tensor_scalar(posm, posm, -1.0, None, ALU.add), counts_ready)

            def count(e):
                a = cnt[0:1, e:e + 1] if isinstance(e, int) else cnt[0:1, ds(e, 1)]
                return ve.value_load(a.bitcast(I32), min_val=0, max_val=NT)

            def one(t, e):
                return t[:, :, e:e + 1] if isinstance(e, int) else t[:, :, ds(e, 1)]

            def one_hot(e, N):
                n = gather_width(N)
                if not isinstance(e, int) or e > 0:
                    ve.wait_ge(gathered, KD * e)
                TT(Poh[:, 0:3 * n].rearrange("p (t n) -> p t n", n=n),
                   iota[:, 0:n].unsqueeze(1).to_broadcast([P, 3, n]), one(posm, e).to_broadcast([P, 3, n]),
                   ALU.is_equal).then_inc(onehot, 1)

            def one_hot_gated(e, N):
                for i, (s0, m) in enumerate(slot_tiles(N)):
                    nq = P // m
                    if not isinstance(e, int) or e > 0:
                        ve.wait_ge(hot_T_made, UNITS * e)
                    TT(Pg[:, :, i * P:(i + 1) * P].rearrange("p t (q m) -> p t q m", m=m),
                       iota[:, s0:s0 + m].unsqueeze(1).unsqueeze(1).to_broadcast([P, 3, nq, m]),
                       one(posm, e).unsqueeze(3).to_broadcast([P, 3, nq, m]), ALU.is_equal) \
                        .then_inc(hot_copies, unit(N))
                    ve.wait_ge(hot_copies, UNITS * e + unit(N) * (i + 1))
                    hg = Pg[:, :, i * P:(i + 1) * P]
                    TT(hg, hg, one(G, e).to_broadcast([P, 3, P]), ALU.mult).then_inc(onehot_g, unit(N))

            def copy_up(e, N, i):
                m = slot_tiles(N)[i][1]
                ve.wait_ge(up_made, UNITS * e + unit(N) * (i + 1))
                ve.tensor_copy(up_rows[:, 0:KD * m], bank_pair(2, KD * m)).then_inc(up_copied, unit(N))

            def swiglu(e, N, i):
                s0, m = slot_tiles(N)[i]
                nq = P // m
                w = min(KD * m, 512)
                by = unit(N) // parts(m)

                def r(a):
                    return a.rearrange("p (c q m) -> p c q m", q=nq, m=m)

                def bias(t, p):
                    t = one(t[:, 4 * p:4 * p + 4, :] if nq == 1 else t, e)
                    return t.rearrange("p (q c) o -> p c q o", q=nq).to_broadcast([P, w // P, nq, m])

                bg, bu = rows_T_banks(N, i)
                for p in range(parts(m)):
                    n = UNITS * e + unit(N) * i + by * (p + 1)
                    if p or i or not isinstance(e, int) or e > 0:
                        ve.wait_ge(act_ready, n - by)
                    ve.wait_ge(gate_T, n)
                    TT(r(tg[:, 0:w]), r(ps[:, bg + p, 0:w]), bias(bgT, p), ALU.add).then_inc(g_biased, by)
                    ve.wait_ge(g_biased, n)
                    ve.tensor_scalar(tg[:, 0:w], tg[:, 0:w], LIMIT, None, ALU.min).then_inc(g_clipped, by)
                    ve.wait_ge(up_T, n)
                    TT(r(tu[:, 0:w]), r(ps[:, bu + p, 0:w]), bias(buT, p), ALU.add).then_inc(u_biased, by)
                    ve.wait_ge(u_biased, n)
                    ve.tensor_scalar(tu[:, 0:w], tu[:, 0:w], LIMIT, -LIMIT, ALU.min, ALU.max).then_inc(u_clipped, by)
                    ve.wait_ge(g_sig, n)
                    TT(sg[:, 0:w], sg[:, 0:w], tg[:, 0:w], ALU.mult).then_inc(glu, by)
                    ve.wait_ge(glu, n)
                    ve.wait_ge(u_clipped, n)
                    a = KD * s0 + p * 512
                    ve.scalar_tensor_tensor(actT[:, a:a + w], tu[:, 0:w], 1.0, sg[:, 0:w], ALU.add, ALU.mult) \
                        .then_inc(act_ready, by)

            def tiles_up(e, N):
                for i in range(len(slot_tiles(N))):
                    copy_up(e, N, i)
                    swiglu(e, N, i)

            def add_up(e):
                for c in range(0, KD, 2):
                    b = comb_bank(c)
                    ve.wait_ge(comb_made, KD * e + c + 2)
                    ve.wait_ge(acc_ready, KD * (e + 1) + c)
                    TT(acc[:, c:c + 2, :], acc[:, c:c + 2, :], ps[:, b:b + 2, 0:NT], ALU.add).then_inc(acc_ready, 2)

            by_width(ve, count(0), lambda N: one_hot(0, N))

            def expert(e, first, last):
                n = count(e)
                by_width(ve, n, lambda N: one_hot_gated(e, N))
                if not last:
                    n1 = count(e + 1)
                    by_width(ve, n1, lambda N: one_hot(e + 1, N))
                if not first:
                    add_up(e - 1)
                by_width(ve, n, lambda N: tiles_up(e, N))

            expert(0, True, False)
            with ve.Fori(1, NEXP - 1) as e:
                expert(e, False, False)
            expert(NEXP - 1, False, True)
            add_up(NEXP - 1)
            ve.wait_ge(acc_ready, KD * (NEXP + 1))
            samp_acc = samp(acc)
            go(TT(samp_acc, samp_acc, per_seq(mods[:, 40:48, 1:9]), ALU.mult))
            go(TT(xT[:, :, SEQ:NT], xT[:, :, SEQ:NT], acc[:, :, SEQ:NT], ALU.add))
            for k in range(KD):
                step(ve.scalar_tensor_tensor(xT[:, k, 0:SEQ], acc[:, k, 0:SEQ], mods[:, 40 + k, 0:1], xT[:, k, 0:SEQ],
                                             ALU.mult, ALU.add), x2_ready)
            recip(rstd2, x2_std)
            for k in range(KD):
                step(ve.scalar_tensor_tensor(hT[:, k, :], xT[:, k, :], g_fin[:, k:k + 1], rstd2, ALU.mult, ALU.mult), y_ready)
            

        @block.scalar
        def _(se):

            def go(ins, signal):
                se.wait_ge(signal, step(ins, signal))

            def copy(out, in_, signal):
                return step(se.copy(out, in_), signal)

            se.wait_ge(in_rows, 16 * 11)
            go(se.activation(csig[0:9, :], crow[0:9, :], ACT.Sigmoid), c_sig)
            for k in range(KD):
                se.wait_ge(x_T, k + 1)
                copy(xT[:, k, :], ps[:, (k + 1) % 8, 0:NT], x_copied)
            se.wait_ge(x_copied, KD)

            def squares(src, name, ready=None, order=range(0, KD, 2)):
                for k in order:
                    if ready:
                        se.wait_ge(ready, k + 2)
                    step(se.activation(scratch[:, k:k + 2, :], src[:, k:k + 2, :], ACT.Square), name)

            def load_sqrt():
                se.activation(stat[:, 15:16], eps[:, :], ACT.Sqrt).then_inc(sqrt_loaded, 1)

            def std(dst, b, n, ss, name):
                se.wait_ge(ss, 1)
                go(se.activation(dst, ps[:, b, 0:NT], ACT.Sqrt, bias=eps[:, :], scale=1.0 / n), name)

            se.wait_ge(ones_set, 1)
            squares(xT, x_sq)
            se.wait_ge(silu, 1)
            std(rstd, 2, D, x_ss, x_std)

            def copy_mods(b, i, made):
                se.wait_ge(pieces_used, made)
                if i > 0:
                    se.wait_ge(mods_T, i)
                copy(mod_rows, ps[:, b, :], mods_copied)

            copy_mods(0, 0, KD)
            for c in range(9):
                for t, (t0, tn) in enumerate(TOK_TILES):
                    if t < 2:
                        se.wait_ge(z_made, 2 * c + t + 1)
                    else:
                        se.wait_ge(pieces_used, IN0 + c + 1)
                    b = 1 + (3 * c + t) % 6
                    if t < 2:
                        copy(Z[:, t, c * 256:(c + 1) * 256], ps[:, b, 0:256], z_copied)
                    else:
                        for j in range(4):
                            copy(Z[0:tn, t, c * 256 + 64 * j:c * 256 + 64 * j + 64], ps[32 * j:32 * j + 32, b, 0:64], z_copied)
            for j in range(6):
                if j % 2 == 0:
                    se.wait_ge(bcu_made, j // 2 + 1)
                else:
                    se.wait_ge(pieces_used, IN0 + 9 + j // 2 + 1)
                copy(BCU[:, j, :], ps[:, 1 + j, 0:NT], bcu_copied)
            se.wait_ge(k_stored, 16 * 2)
            for hp in range(PAIRS):
                se.wait_ge(qk_T, hp + 1)
                b = 7 if hp % 2 == 0 else 0
                dst = Z[:, 0:2, :].rearrange("p t (i c) -> p i t c", i=3)[:, 0:2, :, hp * P:(hp + 1) * P]
                copy(dst, ps[:, b, :].rearrange("p (i t c) -> p i t c", i=2, t=2), qk_copied)
            se.wait_ge(conv_rows_T, 1)
            copy(COT[0:NCS, :], ps[0:NCS, 0, 0:CONV], conv_rows)

            blocks = ((0, 128), (128, 256))
            def p_exp(h):
                b = pP[h % 3]
                se.wait_ge(p_max, 2 * (h) + 2)
                for i, (c0, cn) in enumerate(blocks):
                    s = 4 * (h % 3)
                    step(se.activation(b[:, c0:c0 + cn], b[:, c0:c0 + cn], ACT.Exp, bias=stat[:, s + i:s + i + 1],
                                          accum_out=stat[:, s + 2 + i:s + 3 + i]), p_exped)

            def p_out(h):
                hp, a = h // 2, HD * (h % 2)
                se.wait_ge(p_out_made, h + 1)
                copy(hT[a:a + HD, hp, 0:SEQ], ps[a:a + HD, 5 + h % 2, 0:SEQ], p_out_copied)

            p_exp(0)
            for h in range(HEADS):
                if h + 1 < HEADS:
                    p_exp(h + 1)
                se.wait_ge(p_T, h + 1)
                copy(pPT[h % 2], ps[:, 3 + h % 2, 0:384], p_T_copied)
                if h >= 1:
                    p_out(h - 1)
            p_out(HEADS - 1)

            def a_q_blocks(s):
                if isinstance(s, int):
                    src = qb_all[:, s, :]
                else:
                    src = qb_all[:, ds(s, 1), :].rearrange("p o n -> p (o n)")
                if not isinstance(s, int) or s > 0:
                    se.wait_ge(s_made, s)
                se.copy(qb[:, :, 0:QR], src.rearrange("p (g r) -> p g r", r=QR)).then_inc(qb_ready, 1)

            def a_keys(s, c):
                se.wait_ge(k_used, CHUNKS * s + c + 1)
                b = 2 * (c % 2)
                if c < 2:
                    se.copy(KT[c % 2], bank_pair(b, ATT).rearrange("p (h n) -> p h n", n=P)).then_inc(kt_copied_a, 1)
                else:
                    se.copy(KT[c % 2][:, 4:6, :], ps[:, b + 1, 0:256].rearrange("p (h n) -> p h n", h=2)) \
                        .then_inc(kt_copied_a, 1)

            def a_exp(s):
                se.wait_ge(s_neg, s + 1)
                se.activation(sP, sP, ACT.Exp, bias=stat[:, 8:9], accum_out=stat[:, 9:10]).then_inc(s_exp, 1)

            def a_probs(s):
                se.wait_ge(pt_made, s + 1)
                se.copy(PT[:, 0:4, :], ps[:, 4, :].rearrange("p (c n) -> p c n", n=P)).then_inc(pt_copied, 1)
                se.copy(PT[:, 4:CHUNKS, :], ps[:, 7, 0:384].rearrange("p (c n) -> p c n", n=P)).then_inc(pt_copied, 1)
                se.copy(PT[0:NSAMP, CHUNKS, :], ps[0:NSAMP, 7, 384:512]).then_inc(pt_copied, 1)

            se.wait_ge(conv_stored, 16 * 2)
            copy_mods(7, 1, OUT0 - KD)
            copy_mods(0, 2, OUT0)
            se.wait_ge(qb_zero, 2)
            se.wait_ge(qb_made, 2 * HPS)
            a_q_blocks(0)
            for c in range(CHUNKS):
                a_keys(0, c)

            def sequence(s):
                a_q_blocks(s + 1)
                for c in range(CHUNKS):
                    a_keys(s + 1, c)
                    if c == 1:
                        a_exp(s)
                    if c == 3:
                        a_probs(s)

            sequence(0)
            with se.Fori(1, NSEQ - 1) as s:
                sequence(s)
            a_exp(NSEQ - 1)
            a_probs(NSEQ - 1)

            load_sqrt()
            se.wait_ge(o_copied, 2 * HPS * NSEQ)
            se.wait_ge(conv_stored, 16 * 2)
            squares(hT, cat_sq, order=(6, 0, 2, 4))
            std(rstd_c, 1, CONV, conv_ss, conv_std)
            std(rstd, 0, ATT, att_ss, att_std)
            squares(xT, x1_sq, x1_ready)
            std(rstd2, 1, D, x1_ss, x1_std)
            se.wait_ge(logits_T, 1)
            copy(GT[0:NEXP, :], ps[0:NEXP, 2, 0:NT], logits_copied)
            for t, (t0, tn) in enumerate(TOK_TILES):
                se.wait_ge(gates_less_max, t + 1)
                step(se.activation(gates[0:tn, t, :], gates[0:tn, t, :], ACT.Exp, accum_out=gsum[0:tn, t:t + 1]), gates_exp)
            se.wait_ge(moe_zeros, 1)
            for i in range(6):
                t, j = i // 2, i % 2
                tn = TOK_TILES[t][1]
                se.wait_ge(h2_T, i + 1)
                copy(h2tok[0:tn, t, j * 512:(j + 1) * 512], ps[0:tn, 3 + i % 4, :], h2_copied)
            se.wait_ge(places_made, 1)
            copy(GT[0:NEXP, :], ps[0:NEXP, 1, 0:NT], gates_T)
            se.wait_ge(counts_ready, 1)

            def count(e):
                a = cnt[0:1, e:e + 1] if isinstance(e, int) else cnt[0:1, ds(e, 1)]
                return se.value_load(a.bitcast(I32), min_val=0, max_val=NT)

            def copy_x(e, N):
                n = gather_width(N)
                per = gather_chunks(n)
                for g in range(0, KD, per):
                    se.wait_ge(gathered, KD * e + g + per)
                    se.copy(xe[:, g * n:(g + per) * n], ps[:, 6 + (g // per) % 2, 0:per * n]).then_inc(xe_ready, per)

            def copy_gate(e, N, i):
                m = slot_tiles(N)[i][1]
                se.wait_ge(gate_made, UNITS * e + unit(N) * (i + 1))
                se.copy(gate_rows[:, 0:KD * m], bank_pair(0, KD * m)).then_inc(gate_copied, unit(N))

            def sigmoids(e, N, i):
                m = slot_tiles(N)[i][1]
                w = min(KD * m, 512)
                by = unit(N) // parts(m)
                for p in range(parts(m)):
                    se.wait_ge(g_clipped, UNITS * e + unit(N) * i + by * (p + 1))
                    se.activation(sg[:, 0:w], tg[:, 0:w], ACT.Sigmoid, scale=ALPHA).then_inc(g_sig, by)

            def copy_hot(e, N):
                for i, (s0, m) in enumerate(slot_tiles(N)):
                    se.wait_ge(hot_T_made, UNITS * e + unit(N) * (i + 1))
                    for q in range(P // m):
                        r = slice(q * m, (q + 1) * m)
                        se.copy(bd_tile(m, i)[r, q, :], ps[r, 4 + i % 2, 0:NT]).then_inc(hot_T_ready, unit(N) * m // P)

            def copy_y(e, N):
                for i, (s0, m) in enumerate(slot_tiles(N)):
                    se.wait_ge(down_made, UNITS * e + unit(N) * (i + 1))
                    se.copy(ye[:, i, 0:KD * m], bank_pair(4, KD * m)).then_inc(ye_ready, unit(N))

            def gates_of(e, N):
                tiles = slot_tiles(N)
                for i in range(len(tiles)):
                    copy_gate(e, N, i)
                    if i < len(tiles) - 1:
                        sigmoids(e, N, i)

            by_width(se, count(0), lambda N: copy_x(0, N))
            for c in range(KD):
                se.wait_ge(acc0_made, c + 1)
                copy(acc[:, c, :], ps[:, comb_bank(c), 0:NT], acc_ready)

            def expert(e, last):
                n = count(e)
                by_width(se, n, lambda N: (gates_of(e, N), copy_hot(e, N), sigmoids(e, N, len(slot_tiles(N)) - 1)))
                if not last:
                    n1 = count(e + 1)
                    by_width(se, n1, lambda N: copy_x(e + 1, N))
                by_width(se, n, lambda N: copy_y(e, N))

            with se.Fori(0, NEXP - 1) as e:
                expert(e, False)
            expert(NEXP - 1, True)

            load_sqrt()
            squares(xT, x2_sq, x2_ready)
            std(rstd2, 0, D, x2_ss, x2_std)
            for i in range(6):
                j, t = divmod(i, 3)
                tn = TOK_TILES[t][1]
                se.wait_ge(y_T, i + 1)
                copy(ytok[0:tn, t, j * 512:(j + 1) * 512], ps[0:tn, 1 + 2 * t + j, :], y_copied)


_INS = ["x_prompt", "x_sample", "cache_k", "cache_v", "state_conv", "c_prompt", "c_sample", "w_ada", "b_ada",
        "g_norm_mix", "w_in", "conv_w", "g_attn_out", "g_conv_out", "w_out", "g_norm_ffn", "w_router", "b_router",
        "w_gate", "b_gate", "w_up", "b_up", "w_down", "b_down", "g_final"]
_OUTS = [(1, SEQ, D), (NSEQ, TS, D), (1, 1, SEQ, HEADS, HD), (1, 1, SEQ, HEADS, HD), (1, 1, 2, CONV),
         (1, NSEQ, TS, HEADS, HD), (1, NSEQ, TS, HEADS, HD), (1, NSEQ, 2, CONV)]


def constants():
    import numpy as np

    def log_count(dist):
        n = sum(((dist >= 0) & (dist <= w) & (dist % d == 0)).astype(np.int64) for w, d in ((128, 1), (512, 4), (2048, 16)))
        return np.where(n > 0, np.log(np.maximum(n, 1)), NEG).astype(np.float32)

    out = {"c_ident": np.eye(P, dtype=np.float32),
           "c_tri": np.triu(np.ones((P, P), np.float32), 1),
           "c_iota": np.broadcast_to(np.arange(NT, dtype=np.float32), (P, NT))}
    half = HD // 2
    inv = np.float32(10000.0) ** (-np.arange(half, dtype=np.float32) / np.float32(half))
    rope = np.zeros((P, 3, 2, HD), np.float32)
    for t in range(3):
        pos = P * t + np.arange(P) if t < 2 else PAST + np.arange(P) % TS
        ang = pos.astype(np.float32)[:, None] * inv[None, :]
        cos, sin = np.cos(ang), np.sin(ang)
        rope[:, t, 0] = np.concatenate([cos, cos], 1)
        rope[:, t, 1] = np.concatenate([-sin, sin], 1)
    out["c_rope"] = rope
    q, k = np.arange(P)[:, None], np.arange(P)[None, :]
    out["c_lcp"] = np.concatenate([log_count(q - k), log_count(q + P - k), log_count(q - k)], 1)
    t = np.arange(P)[:, None] % TS
    p = np.arange(P)
    key = [PAST - 512 + c * P + p for c in range(RECENT)] + \
          [((c * P + p) // 4) * 16 + p % 4 for c in range(CHUNKS - RECENT)]
    out["c_lcs"] = log_count(PAST + t - np.concatenate(key)[None, :])
    new = np.full((P, NSEQ, NSAMP), NEG, np.float32)
    for s in range(NSEQ):
        new[:, s, TS * s:TS * s + TS] = log_count(t - np.arange(TS)[None, :])
    out["c_lcn"] = new
    return out


def kernel(**inputs):
    import numpy as np
    import concourse.bacc as bacc
    from concourse.bass_utils import run_bass_kernel_spmd

    nc = bacc.Bacc("TRN2", target_bir_lowering=False, num_devices=1)
    arrays, args = {}, []
    for name, a in [(n, inputs[n]) for n in _INS] + list(constants().items()):
        a = np.ascontiguousarray(a)
        arrays[f"in_{name}"] = a
        args.append(nc.dram_tensor(f"in_{name}", a.shape, mybir.dt.from_np(a.dtype), kind="ExternalInput").ap())
    for i, shape in enumerate(_OUTS):
        args.append(nc.dram_tensor(f"out_{i}", shape, F32, kind="ExternalOutput").ap())
    program(nc, *args)
    r = run_bass_kernel_spmd(nc, [arrays], core_ids=[0])
    return tuple(r.results[0][f"out_{i}"] for i in range(len(_OUTS)))
```
